# Optimizing a Trainium2 kernel written in Bass

```python
import math
import jax, jax.numpy as jnp
from jax import lax
import numpy as np

D_MODEL = 2048
BATCH = 1
SEQ = 128
DEPTH = 1
DEC_BATCH = 1
DEC_SEQ = 512
PAST_LEN = 128

GRID_W = 64
HEAD_DIM = 128
GQA_Q_HEADS = D_MODEL // 256
GQA_KV_HEADS = GQA_Q_HEADS // 4
GQA_GROUP = GQA_Q_HEADS // GQA_KV_HEADS
DIFF_HEADS = D_MODEL // 512
DIFF_V_DIM = 2 * HEAD_DIM
GQA_Q_W = GQA_Q_HEADS * HEAD_DIM
GQA_KV_W = GQA_KV_HEADS * HEAD_DIM
DIFF_QK_W = DIFF_HEADS * 2 * HEAD_DIM
DIFF_V_W = DIFF_HEADS * DIFF_V_DIM
GATE_W = 2 * D_MODEL
PROJ_W = GQA_Q_W + 2 * GQA_KV_W + 2 * DIFF_QK_W + DIFF_V_W + GATE_W
Q_BLOCK = 128
ROPE_THETA = 10000.0
ROPE_PAIRS_PER_AXIS = HEAD_DIM // 4
PEER_HEADS = 8
PEER_N_KEYS = 128
PEER_N_EXPERTS = PEER_N_KEYS * PEER_N_KEYS
PEER_QUERY_DIM = 256
PEER_HALF = PEER_QUERY_DIM // 2
PEER_TOPK = 16
PEER_TOKEN_BLOCK = 128
NORM_EPS = 1e-6

kernel_name = "hybrid_gqa_diffattn_peer_diffusion_step"

def rms_norm(x, g):
    xf = x.astype(jnp.float32)
    y = xf * lax.rsqrt(jnp.mean(xf * xf, axis=-1, keepdims=True) + NORM_EPS)
    return (y * g.astype(jnp.float32)).astype(x.dtype)

def axial_rope_tables(n_tokens):
    rows = n_tokens // GRID_W
    row = jnp.repeat(jnp.arange(rows, dtype=jnp.float32), GRID_W)
    col = jnp.tile(jnp.arange(GRID_W, dtype=jnp.float32), rows)
    inv = ROPE_THETA ** (-jnp.arange(ROPE_PAIRS_PER_AXIS, dtype=jnp.float32) / ROPE_PAIRS_PER_AXIS)
    ar = row[:, None] * inv
    ac = col[:, None] * inv
    ang = jnp.concatenate([ar, ar, ac, ac], axis=-1)
    return jnp.cos(ang), jnp.sin(ang)

def apply_rope(x, cos, sin):
    shape = (1, cos.shape[0]) + (1,) * (x.ndim - 3) + (cos.shape[1],)
    c = cos.reshape(shape).astype(x.dtype)
    s = sin.reshape(shape).astype(x.dtype)
    x1, x2, x3, x4 = jnp.split(x, 4, axis=-1)
    rot = jnp.concatenate([-x2, x1, -x4, x3], axis=-1)
    return x * c + rot * s

def gqa_attention(q, k, v):
    B, Tq = q.shape[:2]
    nb = Tq // Q_BLOCK
    qb = q.reshape(B, nb, Q_BLOCK, GQA_KV_HEADS, GQA_GROUP, HEAD_DIM).transpose(1, 0, 2, 3, 4, 5)
    scale = HEAD_DIM ** -0.5

    def block(qblk):
        s = jnp.einsum('bqhgd,bkhd->bhgqk', qblk, k, preferred_element_type=jnp.float32) * scale
        p = jax.nn.softmax(s, axis=-1).astype(v.dtype)
        return jnp.einsum('bhgqk,bkhd->bqhgd', p, v)

    o = lax.map(block, qb)
    return o.transpose(1, 0, 2, 3, 4, 5).reshape(B, Tq, GQA_Q_W)

def diff_attention(q, k, v, lam):
    B, Tq = q.shape[:2]
    nb = Tq // Q_BLOCK
    qb = q.reshape(B, nb, Q_BLOCK, DIFF_HEADS, 2, HEAD_DIM).transpose(1, 0, 2, 3, 4, 5)
    scale = HEAD_DIM ** -0.5

    def block(qblk):
        s = jnp.einsum('bqhcd,bkhcd->bhcqk', qblk, k, preferred_element_type=jnp.float32) * scale
        p = jax.nn.softmax(s, axis=-1)
        a = (p[:, :, 0] - lam * p[:, :, 1]).astype(v.dtype)
        return jnp.einsum('bhqk,bkhe->bqhe', a, v)

    o = lax.map(block, qb)
    return o.transpose(1, 0, 2, 3, 4).reshape(B, Tq, DIFF_HEADS, DIFF_V_DIM)

def peer_layer(h, w_query, sub_keys, expert_u, expert_v):
    B, T, D = h.shape
    n = B * T
    xt = h.reshape(n, D)
    q = (xt @ w_query).reshape(n, PEER_HEADS, 2, PEER_HALF)
    s = jnp.einsum('nhcd,hckd->nhck', q, sub_keys, preferred_element_type=jnp.float32)
    s1, i1 = lax.top_k(s[:, :, 0], PEER_TOPK)
    s2, i2 = lax.top_k(s[:, :, 1], PEER_TOPK)
    cand_s = (s1[..., :, None] + s2[..., None, :]).reshape(n, PEER_HEADS, PEER_TOPK * PEER_TOPK)
    cand_i = (i1[..., :, None] * PEER_N_KEYS + i2[..., None, :]).reshape(n, PEER_HEADS, PEER_TOPK * PEER_TOPK)
    top_s, pos = lax.top_k(cand_s, PEER_TOPK)
    idx = jnp.take_along_axis(cand_i, pos, axis=-1)
    wts = jax.nn.softmax(top_s, axis=-1)
    nb = n // PEER_TOKEN_BLOCK

    def block(args):
        xb, ib, wb = args
        u = jnp.take(expert_u, ib, axis=0)
        a = jax.nn.gelu(jnp.einsum('nd,nhkd->nhk', xb, u, preferred_element_type=jnp.float32), approximate=False)
        coef = (a * wb).astype(xb.dtype)
        return jnp.einsum('nhk,nhkd->nd', coef, jnp.take(expert_v, ib, axis=0))

    out = lax.map(block, (xt.reshape(nb, PEER_TOKEN_BLOCK, D),
                          idx.reshape(nb, PEER_TOKEN_BLOCK, PEER_HEADS, PEER_TOPK),
                          wts.reshape(nb, PEER_TOKEN_BLOCK, PEER_HEADS, PEER_TOPK)))
    return out.reshape(B, T, D)

def trunk_layer(x, cond, p, layer_idx, rope=None, ctx=None):
    B, T, _ = x.shape
    mod = jax.nn.silu(cond) @ p['w_ada'] + p['b_ada']
    sh1, sc1, g1, sh2, sc2, g2 = [m[:, None, :] for m in jnp.split(mod, 6, axis=-1)]

    h = rms_norm(x, p['norm1_g']) * (1 + sc1) + sh1
    z = h @ p['w_in']
    sizes = (GQA_Q_W, GQA_KV_W, GQA_KV_W, DIFF_QK_W, DIFF_QK_W, DIFF_V_W, GATE_W)
    points = np.cumsum(sizes)[:-1].tolist()
    q_g, k_g, v_g, q_d, k_d, v_d, gate_logits = jnp.split(z, points, axis=-1)
    q_g = rms_norm(q_g.reshape(B, T, GQA_Q_HEADS, HEAD_DIM), p['q_norm_g'])
    k_g = rms_norm(k_g.reshape(B, T, GQA_KV_HEADS, HEAD_DIM), p['k_norm_g'])
    v_g = v_g.reshape(B, T, GQA_KV_HEADS, HEAD_DIM)
    q_d = q_d.reshape(B, T, DIFF_HEADS, 2, HEAD_DIM)
    k_d = k_d.reshape(B, T, DIFF_HEADS, 2, HEAD_DIM)
    v_d = v_d.reshape(B, T, DIFF_HEADS, DIFF_V_DIM)
    own = (k_g, v_g, k_d, v_d)

    if rope is None:
        keys_g, vals_g, keys_d, vals_d = own
    else:
        cos, sin = rope
        q_g = apply_rope(q_g, cos, sin)
        q_d = apply_rope(q_d, cos, sin)
        ck_g, cv_g, ck_d, cv_d = ctx
        keys_g = jnp.concatenate([apply_rope(k_g, cos, sin), ck_g], axis=1)
        vals_g = jnp.concatenate([v_g, cv_g], axis=1)
        keys_d = jnp.concatenate([apply_rope(k_d, cos, sin), ck_d], axis=1)
        vals_d = jnp.concatenate([v_d, cv_d], axis=1)

    o_g = gqa_attention(q_g, keys_g, vals_g)
    lam_init = 0.8 - 0.6 * math.exp(-0.3 * layer_idx)
    lam = (jnp.exp(jnp.sum((p['lq1'] * p['lk1']).astype(jnp.float32)))
           - jnp.exp(jnp.sum((p['lq2'] * p['lk2']).astype(jnp.float32))) + lam_init)
    o_d = diff_attention(q_d, keys_d, vals_d, lam)
    o_d = (rms_norm(o_d, p['subln_g']) * (1 - lam_init)).reshape(B, T, DIFF_V_W)

    gate_a, gate_b = jnp.split(jax.nn.sigmoid(gate_logits), 2, axis=-1)
    merged = gate_a * (o_g @ p['w_branch_a']) + gate_b * (o_d @ p['w_branch_b'])
    x = x + g1 * (merged @ p['w_out'])

    h2 = rms_norm(x, p['norm2_g']) * (1 + sc2) + sh2
    x = x + g2 * peer_layer(h2, p['peer_w_query'], p['peer_sub_keys'], p['peer_u'], p['peer_v'])
    return x, own

def setup_inputs(seed: int = 0) -> dict:
    key = jax.random.key(seed)
    ks = jax.random.split(key, 32)
    f32 = jnp.float32
    D = D_MODEL

    def nrm(k, shape, scale):
        return jax.random.normal(k, shape, f32) * scale

    return {
        'x_prompt': nrm(ks[0], (BATCH, SEQ, D), 1.0),
        'x_sample': nrm(ks[1], (DEC_BATCH, DEC_SEQ, D), 1.0),
        'c': nrm(ks[2], (DEC_BATCH, D), 1.0),
        'cache_gqa_k': nrm(ks[3], (DEC_BATCH, DEPTH, PAST_LEN, GQA_KV_HEADS, HEAD_DIM), 1.0),
        'cache_gqa_v': nrm(ks[4], (DEC_BATCH, DEPTH, PAST_LEN, GQA_KV_HEADS, HEAD_DIM), 1.0),
        'cache_diff_k': nrm(ks[5], (DEC_BATCH, DEPTH, PAST_LEN, DIFF_HEADS, 2, HEAD_DIM), 1.0),
        'cache_diff_v': nrm(ks[6], (DEC_BATCH, DEPTH, PAST_LEN, DIFF_HEADS, DIFF_V_DIM), 1.0),
        'c_ctx': nrm(ks[7], (D,), 1.0),
        'w_ada': nrm(ks[8], (DEPTH, D, 6 * D), 0.5 * D ** -0.5),
        'b_ada': nrm(ks[9], (DEPTH, 6 * D), 0.01),
        'norm1_g': 1.0 + nrm(ks[10], (DEPTH, D), 0.02),
        'norm2_g': 1.0 + nrm(ks[11], (DEPTH, D), 0.02),
        'w_in': nrm(ks[12], (DEPTH, D, PROJ_W), D ** -0.5),
        'q_norm_g': 1.0 + nrm(ks[13], (DEPTH, HEAD_DIM), 0.02),
        'k_norm_g': 1.0 + nrm(ks[14], (DEPTH, HEAD_DIM), 0.02),
        'lambda_q1': nrm(ks[15], (DEPTH, HEAD_DIM), 0.1),
        'lambda_k1': nrm(ks[16], (DEPTH, HEAD_DIM), 0.1),
        'lambda_q2': nrm(ks[17], (DEPTH, HEAD_DIM), 0.1),
        'lambda_k2': nrm(ks[18], (DEPTH, HEAD_DIM), 0.1),
        'diff_subln_g': 1.0 + nrm(ks[19], (DEPTH, DIFF_V_DIM), 0.02),
        'w_branch_a': nrm(ks[20], (DEPTH, GQA_Q_W, D), GQA_Q_W ** -0.5),
        'w_branch_b': nrm(ks[21], (DEPTH, DIFF_V_W, D), DIFF_V_W ** -0.5),
        'w_out': nrm(ks[22], (DEPTH, D, D), D ** -0.5),
        'peer_w_query': nrm(ks[23], (DEPTH, D, PEER_HEADS * PEER_QUERY_DIM), D ** -0.5),
        'peer_sub_keys': nrm(ks[24], (DEPTH, PEER_HEADS, 2, PEER_N_KEYS, PEER_HALF), PEER_HALF ** -0.5),
        'peer_u': nrm(ks[25], (DEPTH, PEER_N_EXPERTS, D), D ** -0.5),
        'peer_v': nrm(ks[26], (DEPTH, PEER_N_EXPERTS, D), PEER_HEADS ** -0.5),
        'final_norm_g': 1.0 + nrm(ks[27], (D,), 0.02),
    }

def reference(x_prompt, x_sample, c, cache_gqa_k, cache_gqa_v, cache_diff_k, cache_diff_v,
              c_ctx, w_ada, b_ada, norm1_g, norm2_g, w_in, q_norm_g, k_norm_g,
              lambda_q1, lambda_k1, lambda_q2, lambda_k2, diff_subln_g,
              w_branch_a, w_branch_b, w_out, peer_w_query, peer_sub_keys, peer_u, peer_v,
              final_norm_g):
    rope = axial_rope_tables(x_sample.shape[1])
    xp = x_prompt
    xs = x_sample
    new_k_g, new_v_g, new_k_d, new_v_d = [], [], [], []
    for l in range(DEPTH):
        p = {
            'w_ada': w_ada[l], 'b_ada': b_ada[l], 'norm1_g': norm1_g[l], 'norm2_g': norm2_g[l],
            'w_in': w_in[l], 'q_norm_g': q_norm_g[l], 'k_norm_g': k_norm_g[l],
            'lq1': lambda_q1[l], 'lk1': lambda_k1[l], 'lq2': lambda_q2[l], 'lk2': lambda_k2[l],
            'subln_g': diff_subln_g[l], 'w_branch_a': w_branch_a[l], 'w_branch_b': w_branch_b[l],
            'w_out': w_out[l], 'peer_w_query': peer_w_query[l], 'peer_sub_keys': peer_sub_keys[l],
            'peer_u': peer_u[l], 'peer_v': peer_v[l],
        }
        xp, (k_g, v_g, k_d, v_d) = trunk_layer(xp, c_ctx[None, :], p, l)
        new_k_g.append(k_g)
        new_v_g.append(v_g)
        new_k_d.append(k_d)
        new_v_d.append(v_d)
        ctx = (cache_gqa_k[:, l], cache_gqa_v[:, l], cache_diff_k[:, l], cache_diff_v[:, l])
        xs, _ = trunk_layer(xs, c, p, l, rope=rope, ctx=ctx)
    y_prompt = rms_norm(xp, final_norm_g)
    y_sample = rms_norm(xs, final_norm_g)
    new_gqa_k = jnp.stack(new_k_g, axis=1)
    new_gqa_v = jnp.stack(new_v_g, axis=1)
    new_diff_k = jnp.stack(new_k_d, axis=1)
    new_diff_v = jnp.stack(new_v_d, axis=1)
    return (y_prompt, y_sample, new_gqa_k, new_gqa_v, new_diff_k, new_diff_v)


_drawn_inputs = setup_inputs


def setup_inputs(seed=0):
    import zlib

    import numpy as np

    out = dict(_drawn_inputs(seed))
    spreads = {}
    factors = {'cache_gqa_k': 8.0,
     'cache_gqa_v': 8.0,
     'b_ada': 4.183,
     'norm1_g': 2.928,
     'norm2_g': 6.502,
     'q_norm_g': 8.0,
     'k_norm_g': 2.854,
     'lambda_q1': 5.671,
     'lambda_k1': 6.016,
     'lambda_q2': 5.544,
     'lambda_k2': 4.753,
     'diff_subln_g': 8.0,
     'final_norm_g': 7.875,
     'cache_diff_k': 8.0,
     'cache_diff_v': 8.0}
    for name, (base, spread) in spreads.items():
        noise = np.random.default_rng([zlib.crc32(name.encode()), seed]).standard_normal(out[name].shape)
        drawn = base * np.exp(spread * noise) if base else spread * noise
        out[name] = __import__('jax').numpy.asarray(drawn.astype(out[name].dtype))
    for name, factor in factors.items():
        out[name] = (out[name] * factor).astype(out[name].dtype)
    return out
```

```python
import math
from contextlib import ExitStack, contextmanager

import numpy as np

import concourse.bass as bass
from concourse import mybir

D = 2048
SEQ = 128
DEC_SEQ = 512
PAST = 128
GRID_W = 64
HD = 128
QH, KVH, DH = 8, 2, 4
VD = 2 * HD
P = 128
KT = D // P
NB = (SEQ + DEC_SEQ) // P
SB = DEC_SEQ // P
CH = 512
PROJ_W = QH * HD + 2 * KVH * HD + 2 * DH * 2 * HD + DH * VD + 2 * D
QG0, KG0, VG0 = 0, QH * HD, (QH + KVH) * HD
QD0 = (QH + 2 * KVH) * HD
KD0 = QD0 + 2 * DH * HD
VD0 = KD0 + 2 * DH * HD
ZW = VD0 + DH * VD
NKH = KVH + 2 * DH
VW = KVH * HD + DH * VD
ADA_CH, QKV_CH, DCH = 6 * D // CH, ZW // CH, D // CH
GROUP = (1, SB)
WS = 3
HALF = KT // 2 * CH
H_QKV = 2 * ADA_CH
H_BR = (H_QKV + 2 * QKV_CH, H_QKV + 2 * QKV_CH + 10 * DCH)
H_OUT = tuple(h + 6 * DCH for h in H_BR)
H_QRY = tuple(h + 2 * DCH for h in H_OUT)
U_BR = (NB * QKV_CH, NB * QKV_CH + 6 * DCH * GROUP[0])
U_OUT = tuple(u + 4 * DCH * g for u, g in zip(U_BR, GROUP))
U_QRY = tuple(u + DCH * g for u, g in zip(U_OUT, GROUP))
T_O = (NB, NB + 3 * GROUP[0])
T_M = tuple(t + g for t, g in zip(T_O, GROUP))
T_H = tuple(t + g for t, g in zip(T_M, GROUP))
EPS = 1e-6
SCALE = HD ** -0.5
LAM_INIT = 0.8 - 0.6 * math.exp(-0.3 * 0)
NEG = -3.0e38
PH, NK, TOPK = 8, 128, 16
STEPS = NB * PH
RINGS = (4, 8)
STEP0 = (0, PH)


class Chain:

    def __init__(self, eng, sem):
        self.eng, self.sem, self.base, self.k = eng, sem, 0, 0

    def link(self, ins):
        ins.then_inc(self.sem, 1)
        self.k += 1
        self.eng.wait_ge(self.sem, self.base + self.k)

    @contextmanager
    def loop(self, n, per):
        start = self.base + self.k
        with self.eng.Fori(0, n) as i:
            self.base, self.k = i * per + start, 0
            yield i
            assert self.k == per, self.k
        self.base, self.k = start + n * per, 0


def build(nc, I, O):
    f32, u32 = mybir.dt.float32, mybir.dt.uint32
    ALU, ACT, AX = mybir.AluOpType, mybir.ActivationFunctionType, mybir.AxisListType
    ds = bass.ds

    mod = nc.dram_tensor("mod_rows", (2, 6 * D), f32).ap()
    zs = nc.dram_tensor("z_blocks", (NB, P, ZW), f32).ap()
    osd = nc.dram_tensor("o_blocks", (NB, P, D), f32).ap()
    md = nc.dram_tensor("merged_blocks", (NB, P, D), f32).ap()
    x1d = nc.dram_tensor("x1_blocks", (NB, P, D), f32).ap()
    h2d = nc.dram_tensor("h2_blocks", (SB, P, D), f32).ap()
    scd = nc.dram_tensor("scores", (P, (STEPS + 1) * VD), f32).ap()

    xs = I["x_sample"].rearrange("a (b p) d -> (a b) p d", p=P)
    xp = I["x_prompt"].rearrange("a (b p) d -> (a b) p d", p=P)
    ys = O[1].rearrange("a (b p) d -> (a b) p d", p=P)
    yp = O[0].rearrange("a (b p) d -> (a b) p d", p=P)
    w_ada = I["w_ada"].rearrange("l (p t) n -> p (l t) n", p=P)
    w_in = I["w_in"].rearrange("l (t p) n -> p (l t) n", p=P)
    w_a = I["w_branch_a"].rearrange("l (t p) n -> p (l t) n", p=P)
    w_b = I["w_branch_b"].rearrange("l (t p) n -> p (l t) n", p=P)
    w_out = I["w_out"].rearrange("l (t p) n -> p (l t) n", p=P)
    w_qry = I["peer_w_query"].rearrange("l (t p) n -> p (l t) n", p=P)
    eu = I["peer_u"].rearrange("l e d -> (l e) d")
    ev = I["peer_v"].rearrange("l e d -> (l e) d")
    sub = I["peer_sub_keys"].rearrange("l h c k d -> k (l h c) d")
    ckg = I["cache_gqa_k"].rearrange("a l s h d -> (a l s) (h d)")
    cvg = I["cache_gqa_v"].rearrange("a l s h d -> (a l s) (h d)")
    ckd = I["cache_diff_k"].rearrange("a l s h c d -> (a l s) (h c d)")
    cvd = I["cache_diff_v"].rearrange("a l s h d -> (a l s) (h d)")
    nkg = O[2].rearrange("a l s h d -> (a l s) (h d)")
    nvg = O[3].rearrange("a l s h d -> (a l s) (h d)")
    nkd = O[4].rearrange("a l s h c d -> (a l s) (h c d)")
    nvd = O[5].rearrange("a l s h d -> (a l s) (h d)")

    ctx = ExitStack()
    with ctx:
        def sb(name, shape, dt=f32):
            return ctx.enter_context(nc.sbuf_tensor(name, shape, dt))

        def sem(name):
            return ctx.enter_context(nc.semaphore(name))

        act = sb("activations", [P, 2 * SB * D])
        big = sb("big", [P, WS * HALF + 6 * D])
        zone = sb("zone", [P, 2 * D])
        zt_f = sb("zt", [P, NB * CH])
        misc = sb("misc", [P, D])
        ident = sb("ident", [P, P])
        qts = sb("qts", [P, CH])
        small = sb("small", [P, 96])
        iota16 = sb("iota16", [P, TOPK])
        sel = sb("sel", [P, 2, TOPK], u32)
        work = sb("work", [P, 1872])
        ps = ctx.enter_context(nc.psum_tensor("ps", [P, 8 * 512], f32))

        A1 = SB * D
        G0 = WS * HALF
        W0 = 0

        def ac(lo, n):
            return act[:, lo:lo + n]

        def bg(lo, n):
            return big[:, lo:lo + n]

        def zn(lo, n):
            return zone[:, lo:lo + n]

        def bank(b, n=512):
            return ps[:, b * 512:b * 512 + n]

        def wk(lo, n):
            return work[:, lo:lo + n]

        def tiles(ap):
            return ap.rearrange("p (k n) -> p k n", k=KT)

        w = bg(W0, WS * HALF).rearrange("p (s k n) -> p s k n", s=WS, k=KT // 2)
        zt = zt_f[:, :].rearrange("p (b n) -> p b n", b=NB)
        acc, hcur = bg(G0 + 4 * D, D), bg(G0 + 5 * D, D)
        a0, a1 = tiles(ac(0, SB * D)), tiles(ac(A1, SB * D))
        hT = (tiles(bg(G0, D)), a0)
        oT = (tiles(ac(A1, D)), a1)
        mT = (tiles(ac(A1 + D, D)), a0)
        h2T = (tiles(ac(A1 + 2 * D, D)), a0)
        nbuf = (((ac(A1 + 3 * D, D),), hcur, zn(0, D), zn(D, D), acc),
                ((ac(A1, D), ac(A1 + D, D)), ac(A1 + 2 * D, D), ac(A1 + 3 * D, D), zn(0, D), zn(D, D)))
        KTB, PTB, QB, VB = A1, A1 + 6400, G0 + 4 * D + 256, G0 + D
        onat, tmp4, subg = zn(0, D), zn(D, DH * VD), zn(D + DH * VD, VD)
        QZ, QT = A1, A1 + NB * CH + 2 * CH
        sc2, rep = wk(0, 256), wk(256, 256)
        vals, valsi = wk(512, 32), wk(544, 32).bitcast(u32)
        cand, cand2 = wk(576, 256), wk(832, 256)
        candi, top = wk(1088, 16).bitcast(u32), wk(1104, 16)
        hl = wk(1120, 32).bitcast(u32)
        hlf, vif = wk(1152, 32), wk(1184, 32)
        oh = wk(1216, 512)
        eidx = wk(1728, 32)
        ex16, gel, dots, coef = wk(1760, 16), wk(1776, 16), wk(1792, 16), wk(1808, 16)
        wts = wk(1824, 32)
        ntop, exsum, rsum = wk(1856, 1), wk(1857, 1), wk(1858, 1)

        def slot(g, j):
            return bg((G0 if g == 0 else W0) + (j % RINGS[g]) * D, D)

        w_in_sem = [sem(f"w_loaded{i}") for i in range(WS)]
        w_free = sem("w_free")
        const_ready, ident0, pad_out = sem("const_ready"), sem("ident0"), sem("pad_out")
        dve_s = sem("dve_self")
        mm_done, bank_free = sem("mm_done"), sem("bank_free")
        t_done, t_free = sem("t_done"), sem("t_free")
        cond_in, cond_sig, cond_ready = sem("cond_in"), sem("cond_sig"), sem("cond_ready")
        bada_in, ada_mm, ada_free, ada_out = sem("bada_in"), sem("ada_mm"), sem("ada_free"), [sem(f"ada_out{i}") for i in range(3)]
        nrm = [dict(x=[sem(f"n{s}_x{i}") for i in range(2)], row=sem(f"n{s}_row"), h=sem(f"n{s}_h"), base=base)
               for s, base in enumerate((NB, NB + 1, 0))]
        nrm_ms, nrm_rs, h2_out = sem("norm_ms"), sem("norm_rs"), sem("h2_out")
        qk_tab, qn_ms, qn_rs, zo_ready = sem("qk_tab"), sem("qn_ms"), sem("qn_rs"), sem("zo_ready")
        zo_out = [sem(f"zo_out{b}") for b in range(NB)]
        att = [dict(kn=[sem(f"a{s}_kn{i}") for i in range(2)], kt=sem(f"a{s}_kt"), ke=sem(f"a{s}_ke"), v=sem(f"a{s}_v"))
               for s in range(2)]
        for name in ("q", "qt", "qe", "sc", "nm", "ex", "pn", "pt", "pe", "pv", "oe", "ms", "rs", "o", "st"):
            att[0][name] = att[1][name] = sem("att_" + name)
        lam_in, lam_dot, lam_exp = sem("lam_in"), sem("lam_dot"), sem("lam_exp")
        sk_in, sk_t, sk_e = sem("sk_in"), sem("sk_t"), sem("sk_e")
        grp = [dict(nat=[sem(f"g{s}_nat{i}") for i in range(2)], gates=sem(f"g{s}_gates_free"), zt=sem(f"g{s}_zt_used"),
                    br=sem(f"g{s}_br_ready"), br_st=[sem(f"g{s}_br_st{i}") for i in range(GROUP[s])],
                    g1=sem(f"g{s}_g1"), xt=[sem(f"g{s}_xt{i}") for i in range(GROUP[s])], ou=sem(f"g{s}_ou_ready"),
                    ou_st=[sem(f"g{s}_ou_st{i}") for i in range(4)], tq=sem(f"g{s}_tq"), te=sem(f"g{s}_te"),
                    sk=sem(f"g{s}_sk"), se=sem(f"g{s}_se"), sc_st=[sem(f"g{s}_sc_st{i}") for i in range(4)])
               for s in range(2)]
        ring_in = [[sem(f"ring{g}_in{i}") for i in range(RINGS[g])] for g in range(2)]
        ring_free = [sem(f"ring{g}_free") for g in range(2)]
        sc_in, sel_ready, tk_neg, tk_exp, ge_done = sem("sc_in"), sem("sel_ready"), sem("tk_neg"), sem("tk_exp"), sem("ge_done")
        fa_in, fx_in, hn_in, h_taken = sem("fa_in"), sem("fx_in"), sem("hn_in"), sem("h_taken")
        f_ms, f_rs, y_ready, y_out, kv_out = sem("f_ms"), sem("f_rs"), sem("y_ready"), sem("y_out"), sem("kv_out")

        block = ctx.enter_context(nc.Block())

        def block_of(g, lb):
            return SB if g == 0 else lb

        def done_output(sc):
            return sc if sc < 8 else 8 + (sc - 9) // 2 if sc % 2 else None

        @block.sync
        def _(sp):
            def half(n, i, step, ap):
                sp.wait_ge(w_free, n + 1 + i * step)
                sp.nop(nofuse=True)
                sp.dma_start(w[:, n % WS], ap).then_inc(w_in_sem[n % WS], 16)

            def part(t, h, at):
                return t[:, h * (KT // 2):(h + 1) * (KT // 2), ds(at, CH)]

            with sp.Fori(0, ADA_CH // 3) as i:
                for j in range(6):
                    half(j, i, 6, part(w_ada, j % 2, i * (3 * CH) + (j // 2) * CH))
            with sp.Fori(0, QKV_CH // 3) as i:
                for j in range(6):
                    half(H_QKV + j, i, 6, part(w_in, j % 2, i * (3 * CH) + (j // 2) * CH))

            for g in range(2):
                n, G, s = GROUP[g], grp[g], nrm[g]

                def br(c, j):
                    at = c * CH
                    return part(w_in, j % 2, at + (ZW if j < 2 else ZW + D)) if j < 4 else part((w_a, w_b)[j - 4], 0, at)

                half(H_BR[g], 0, 0, br(0, 0))
                half(H_BR[g] + 1, 0, 0, br(0, 1))
                for lb in range(n):
                    if lb == 0:
                        sp.wait_ge(att[1]["st"], 16 * NB)
                        if g:
                            for i in range(4):
                                sp.wait_ge(grp[0]["sc_st"][i], 16)
                    if lb >= 2:
                        sp.wait_ge(t_done, 4 * (T_O[g] + lb - 1))
                    sp.dma_start(zn((lb % 2) * D, D), osd[block_of(g, lb)]).then_inc(G["nat"][lb % 2], 16)

                def merged_out(c, i):
                    for lb in range(n):
                        sp.wait_ge(G["br"], i * n + lb + 1)
                        sp.nop(nofuse=True)
                        sp.dma_start(md[block_of(g, lb), :, ds(c * CH, CH)], zn(lb * CH, CH)).then_inc(G["br_st"][lb], 16)

                with sp.Fori(0, DCH - 1) as c:
                    for j in range(2, 6):
                        half(H_BR[g] + j, c, 6, br(c, j))
                    for j in range(2):
                        half(H_BR[g] + 6 + j, c, 6, br(c + 1, j))
                    merged_out(c, c)
                for j in range(2, 6):
                    half(H_BR[g] + 6 * (DCH - 1) + j, 0, 0, br(DCH - 1, j))
                for j in range(2):
                    half(H_OUT[g] + j, 0, 0, part(w_out, j, 0))
                merged_out(DCH - 1, DCH - 1)
                for lb in range(n):
                    sp.wait_ge(G["br_st"][lb], 16 * DCH)
                for lb in range(n):
                    if lb >= 2:
                        sp.wait_ge(t_done, 4 * (T_M[g] + lb - 1))
                    sp.dma_start(zn((lb % 2) * D, D), md[block_of(g, lb)]).then_inc(G["nat"][lb % 2], 16)
                sp.wait_ge(t_done, 4 * (T_M[g] + n))
                cnd = 1 - g
                sp.dma_start(zn(0, D), mod[cnd:cnd + 1, 2 * D:3 * D].to_broadcast([P, D])).then_inc(G["g1"], 16)
                for c in range(DCH):
                    for lb in range(n):
                        if c:
                            sp.wait_ge(G["ou"], (c - 1) * n + lb + 1)
                        src = (xs[lb] if g else xp[0])[:, c * CH:(c + 1) * CH]
                        sp.dma_start(zn(D + lb * CH, CH), src).then_inc(G["xt"][lb], 16)
                    for j in range(2):
                        if c < DCH - 1:
                            half(H_OUT[g] + 2 * (c + 1) + j, 0, 0, part(w_out, j, (c + 1) * CH))
                        else:
                            half(H_QRY[g] + j, 0, 0, part(w_qry, j, 0))
                    for lb in range(n):
                        v = c * n + lb
                        sp.wait_ge(G["ou"], v + 1)
                        sp.dma_start(x1d[block_of(g, lb), :, c * CH:(c + 1) * CH], zt[:, v % 4]).then_inc(G["ou_st"][v % 4], 16)
                for i in range(4):
                    sp.wait_ge(G["ou_st"][i], 16 * n)
                xb, h, A, Bv, gain = nbuf[g]
                sp.dma_start(gain, I["norm2_g"].to_broadcast([P, D])).then_inc(s["row"], 16)
                sp.dma_start(A, mod[cnd:cnd + 1, 4 * D:5 * D].to_broadcast([P, D])).then_inc(s["row"], 16)
                sp.dma_start(Bv, mod[cnd:cnd + 1, 3 * D:4 * D].to_broadcast([P, D])).then_inc(s["row"], 16)
                for lb in range(min(2, n)):
                    sp.dma_start(xb[lb], x1d[block_of(g, lb)]).then_inc(s["x"][lb], 16)
                for lb in range(n):
                    if g:
                        sp.wait_ge(s["h"], lb + 1)
                        sp.dma_start(h2d[lb], h).then_inc(h2_out, 16)
                        if lb + 2 < n:
                            sp.dma_start(xb[lb % 2], x1d[lb + 2]).then_inc(s["x"][lb % 2], 16)
                for c in range(DCH):
                    for j in range(2):
                        if c < DCH - 1:
                            half(H_QRY[g] + 2 * (c + 1) + j, 0, 0, part(w_qry, j, (c + 1) * CH))
                    last = c * n + n if c == DCH - 1 else c * n + n - 2
                    for v in range(max(0, c * n - 2), last):
                        sp.wait_ge(G["se"], v + 1)
                        at = (STEP0[g] + PH * (v % n) + 2 * (v // n)) * VD
                        sp.dma_start(scd[:, at:at + CH], zn((v % 4) * CH, CH)).then_inc(G["sc_st"][v % 4], 16)

            sp.wait_ge(t_done, 4 * (T_H[1] + SB))
            sp.wait_ge(h2_out, 16 * SB)
            sp.dma_start(ac(A1, D), x1d[SB]).then_inc(fa_in, 16)
            sp.dma_start(ac(A1 + D, D), mod[1:2, 5 * D:6 * D].to_broadcast([P, D])).then_inc(fa_in, 16)
            sp.dma_start(ac(A1 + 2 * D, D), I["final_norm_g"].rearrange("(a n) -> a n", a=1).to_broadcast([P, D])).then_inc(fa_in, 16)
            sp.wait_ge(mm_done, U_QRY[1] + DCH * SB)
            sp.dma_start(ac(2 * D, D), h2d[0]).then_inc(hn_in, 16)
            sp.dma_start(ac(0, D), x1d[0]).then_inc(fx_in, 16)
            sp.dma_start(ac(D, D), mod[0:1, 5 * D:6 * D].to_broadcast([P, D])).then_inc(fx_in, 16)
            sp.wait_ge(y_ready, 1)
            sp.dma_start(yp[0], ac(A1, D)).then_inc(y_out, 16)
            for b in range(SB):
                if b + 1 < SB:
                    sp.wait_ge(h_taken, b + 1)
                    sp.dma_start(ac(2 * D, D), h2d[b + 1]).then_inc(hn_in, 16)
                sp.wait_ge(y_ready, b + 2)
                sp.dma_start(ys[b], ac(0, D)).then_inc(y_out, 16)
                sp.wait_ge(y_out, 16 * (b + 2))
                if b + 1 < SB:
                    sp.dma_start(ac(0, D), x1d[b + 1]).then_inc(fx_in, 16)

        @block.gpsimd
        def _(pool):
            pool.dma_start(small[:, 0:16], I["c"].rearrange("a (p t) -> (a p) t", p=P)).then_inc(cond_in, 16)
            pool.dma_start(small[:, 16:32], I["c_ctx"].rearrange("(p t) -> p t", p=P)).then_inc(cond_in, 16)
            pool.dma_start(act[0:2, 0:6 * D], I["b_ada"].to_broadcast([2, 6 * D])).then_inc(bada_in, 16)
            for n, v in enumerate(("lambda_q1", "lambda_k1", "lambda_q2", "lambda_k2")):
                pool.dma_start(misc[:, n * HD:(n + 1) * HD], I[v].to_broadcast([P, HD])).then_inc(lam_in, 16)
            nc.gpsimd.memset(ident[:, :], 0.0).then_inc(ident0, 1)
            pool.wait_ge(ident0, 1)
            nc.gpsimd.affine_select(out=ident[:, :], in_=ident[:, :], compare_op=ALU.not_equal, fill=1.0, base=0,
                                    pattern=[[-1, P]], channel_multiplier=1).then_inc(const_ready, 1)
            nc.gpsimd.iota(iota16[:, :], pattern=[[1, TOPK]], base=0, channel_multiplier=0,
                           allow_small_or_imprecise_dtypes=True).then_inc(const_ready, 1)
            pool.wait_ge(const_ready, 2)
            for i in range(2):
                pool.dma_start(scd[:, STEPS * VD + i * P:STEPS * VD + (i + 1) * P], ident[:, :]).then_inc(pad_out, 16)

            with pool.Fori(0, ADA_CH // 3) as i:
                for j in range(3):
                    pool.wait_ge(ada_free, i * 3 + j + 4)
                    pool.nop(nofuse=True)
                    pool.dma_start(mod[:, ds(i * (3 * CH) + j * CH, CH)], zt[0:2, j]).then_inc(ada_out[j], 16)
            for j in range(3):
                pool.wait_ge(ada_out[j], 16 * (ADA_CH // 3))

            s = nrm[2]
            xb, h, A, Bv, gain = nbuf[1]
            pool.dma_start(gain, I["norm1_g"].to_broadcast([P, D])).then_inc(s["row"], 16)
            for b in range(NB):
                c = 0 if b < SB else 1
                if b in (0, SB):
                    if b:
                        pool.wait_ge(s["h"], b)
                    pool.dma_start(A, mod[c:c + 1, D:2 * D].to_broadcast([P, D])).then_inc(s["row"], 16)
                    pool.dma_start(Bv, mod[c:c + 1, 0:D].to_broadcast([P, D])).then_inc(s["row"], 16)
                if b >= 2:
                    pool.wait_ge(s["h"], b - 1)
                pool.dma_start(xb[b % 2], xs[b] if b < SB else xp[0]).then_inc(s["x"][b % 2], 16)

            pool.wait_ge(s["h"], NB)
            pool.wait_ge(t_done, NB * 4)
            pool.dma_start(ac(QT, SB * HD).rearrange("p (b d) -> p b d", b=SB), I["rope_cos"].rearrange("(b p) d -> p b d", p=P)).then_inc(qk_tab, 16)
            pool.dma_start(ac(QT + SB * HD, SB * HD).rearrange("p (b d) -> p b d", b=SB), I["rope_sin"].rearrange("(b p) d -> p b d", p=P)).then_inc(qk_tab, 16)
            pool.dma_start(ac(QT + 2 * SB * HD, HD), I["q_norm_g"].to_broadcast([P, HD])).then_inc(qk_tab, 16)
            pool.dma_start(ac(QT + 2 * SB * HD + HD, HD), I["k_norm_g"].to_broadcast([P, HD])).then_inc(qk_tab, 16)
            with pool.Fori(0, QKV_CH) as r:
                for b in range(NB):
                    pool.wait_ge(zo_ready, r * NB + b + NB + 1)
                    pool.nop(nofuse=True)
                    pool.dma_start(zs[b, :, ds(r * CH, CH)], ac(QZ + b * CH, CH)).then_inc(zo_out[b], 16)
            for b in range(NB):
                pool.wait_ge(zo_out[b], 16 * QKV_CH)

            for s in range(2):
                a = att[s]
                T, blocks = (SB + 1, SB) if s == 0 else (1, 1)
                if s:
                    pool.wait_ge(att[0]["st"], 16 * SB)
                for t in range(T):
                    if t >= 2:
                        pool.wait_ge(a["kt"], 3 * (t - 1))
                    at = QB + (t % 2) * NKH * HD
                    blk = t if s == 0 else SB
                    cache = s == 0 and t == SB
                    pool.dma_start(bg(at, KVH * HD), ckg if cache else zs[blk, :, KG0:VG0]).then_inc(a["kn"][t % 2], 16)
                    pool.dma_start(bg(at + KVH * HD, 2 * DH * HD), ckd if cache else zs[blk, :, KD0:VD0]).then_inc(a["kn"][t % 2], 16)
                    pool.dma_start(bg(VB + t * VW, KVH * HD), cvg if cache else zs[blk, :, VG0:QD0]).then_inc(a["v"], 16)
                    pool.dma_start(bg(VB + t * VW + KVH * HD, DH * VD), cvd if cache else zs[blk, :, VD0:ZW]).then_inc(a["v"], 16)
                if s == 0:
                    pool.dma_start(subg, I["diff_subln_g"].to_broadcast([P, VD])).then_inc(a["v"], 16)
                    for dst, lo, n in ((nkg, KG0, KVH * HD), (nvg, VG0, KVH * HD), (nkd, KD0, 2 * DH * HD), (nvd, VD0, DH * VD)):
                        pool.dma_start(dst, zs[SB, :, lo:lo + n]).then_inc(kv_out, 16)
                pool.wait_ge(a["kt"], 3 * T)
                for b in range(blocks):
                    blk = b if s == 0 else SB
                    if b:
                        pool.wait_ge(a["qt"], 4 * (s * SB + b))
                    pool.dma_start(bg(QB, QH * HD), zs[blk, :, QG0:KG0]).then_inc(a["q"], 16)
                    pool.dma_start(bg(QB + QH * HD, QH * HD), zs[blk, :, QD0:KD0]).then_inc(a["q"], 16)
                    if b:
                        pool.wait_ge(a["o"], s * SB + b)
                        pool.dma_start(osd[blk - 1], onat).then_inc(a["st"], 16)
                pool.wait_ge(a["o"], s * SB + blocks)
                pool.dma_start(osd[blk], onat).then_inc(a["st"], 16)
            pool.wait_ge(att[1]["st"], 16 * NB)
            pool.dma_start(hcur.rearrange("p (c d) -> p c d", c=2 * PH), sub).then_inc(sk_in, 16)

            def scores_in(step):
                pool.dma_start(sc2, scd[:, ds(step * VD, VD)]).then_inc(sc_in, 16)

            def gathers(g, step, q, at, ahead=True):
                pool.wait_ge(sel_ready, step + 1)
                pool.nop(nofuse=True)
                if ahead:
                    scores_in(step + 1)
                for j in range(2 * TOPK):
                    pool.wait_ge(ring_free[g], at + j + 1)
                    pool.nop(nofuse=True)
                    pool.indirect_dma_start(
                        slot(g, j), None, eu if j < TOPK else ev,
                        bass.IndirectOffsetOnAxis(ap=sel[:, q, j % TOPK:j % TOPK + 1], axis=0)).then_inc(ring_in[g][j % RINGS[g]], 16)

            for g in range(2):
                for i in range(4):
                    pool.wait_ge(grp[g]["sc_st"][i], 16 * GROUP[g])
                if g:
                    pool.wait_ge(pad_out, 32)
                    pool.wait_ge(sel_ready, PH)
                scores_in(STEP0[g])
                steps = PH * GROUP[g]
                with pool.Fori(0, steps // 2 - (1 - g)) as i:
                    for q in range(2):
                        gathers(g, i * 2 + STEP0[g] + q, q, i * (4 * TOPK) + q * 2 * TOPK)
                if g == 0:
                    for q in range(2):
                        gathers(g, PH - 2 + q, q, (PH - 2 + q) * 2 * TOPK, ahead=q == 0)
            pool.wait_ge(kv_out, 16 * 4)

        @block.tensor
        def _(pe):
            def wait_half(n, i, step):
                pe.wait_ge(w_in_sem[n % WS], 16 * (n // WS + 1) + i * (16 * step // WS))

            def products(acts, b, n, bk, start, stop):
                for k in range(KT // 2):
                    ins = nc.tensor.matmul(bank(bk), acts[:, k, b * P:(b + 1) * P], w[:, n % WS, k],
                                           start=(start and k == 0), stop=(stop and k == KT // 2 - 1))
                return ins

            def chunk(acts, n, i, step, blocks, u, bank_of, depth):
                for h in range(2):
                    wait_half(n + h, i, step)
                    for b in range(blocks):
                        if h == 0:
                            pe.wait_ge(bank_free, u + b + 1 + NB - depth)
                        ins = products(acts[:, h * (KT // 2):(h + 1) * (KT // 2)], b, n + h, bank_of(b), h == 0, h == 1)
                        if h == 1:
                            ins.then_inc(mm_done, 1)
                    if h == 0:
                        ins.then_inc(w_free, 1)
                release(u + blocks)

            def release(u):
                pe.wait_ge(mm_done, u)
                pe.sem_inc(w_free, 1)

            def transposes(B, src):
                for q in range(4):
                    pe.wait_ge(t_free, B * 4 + q + 1)
                    for k in range(4):
                        ins = nc.tensor.transpose(ps[:, (4 + q) * 512 + k * P:(4 + q) * 512 + (k + 1) * P],
                                                  src[:, (4 * q + k) * P:(4 * q + k + 1) * P], ident[:, :])
                    ins.then_inc(t_done, 1)

            pe.sem_inc(w_free, WS)
            pe.sem_inc(att[0]["pv"], 2)
            pe.wait_ge(cond_ready, 1)
            cond = small[:, 64:96].rearrange("p (t c) -> p t c", c=2)
            with pe.Fori(0, ADA_CH // 3) as i:
                for j in range(3):
                    pe.wait_ge(ada_free, i * 3 + j + 1)
                    pe.nop(nofuse=True)
                    for h in range(2):
                        wait_half(2 * j + h, i, 6)
                        for k in range(KT // 2):
                            ins = nc.tensor.matmul(ps[0:2, j * 512:(j + 1) * 512], cond[:, h * (KT // 2) + k], w[:, (2 * j + h) % WS, k],
                                                   start=(h + k == 0), stop=(h == 1 and k == KT // 2 - 1))
                        ins.then_inc(ada_mm if h else w_free, 1)
                    pe.wait_ge(ada_mm, i * 3 + j + 1)
                    pe.sem_inc(w_free, 1)
            pe.wait_ge(const_ready, 2)
            for b in range(NB):
                pe.wait_ge(nrm[2]["h"], b + 1)
                transposes(b, nbuf[1][1])
            pe.wait_ge(t_free, NB * 4 + 4)
            pe.wait_ge(ada_free, 3 + ADA_CH)

            with pe.Fori(0, QKV_CH // 3) as i:
                for j in range(3):
                    n, u = H_QKV + 2 * j, i * (3 * NB) + j * NB
                    for h in range(2):
                        wait_half(n + h, i, 6)
                        for b in range(NB):
                            if h == 0:
                                pe.wait_ge(bank_free, u + b + 1)
                            acts = hT[1] if b < SB else hT[0]
                            ins = products(acts[:, h * (KT // 2):(h + 1) * (KT // 2)], b % SB, n + h, b, h == 0, h == 1)
                            if h == 1:
                                ins.then_inc(mm_done, 1)
                        if h == 0:
                            ins.then_inc(w_free, 1)
                    release(u + NB)

            for s in range(2):
                a = att[s]
                T, blocks = (SB + 1, SB) if s == 0 else (1, 1)
                kT = ac(KTB, NKH * T * P).rearrange("p (h n) -> p h n", h=NKH)
                qT = misc[:, :].rearrange("p (h n) -> p h n", h=16)
                if s:
                    pe.wait_ge(att[0]["oe"], 12 * SB + 2)
                for t in range(T):
                    pe.wait_ge(a["kn"][t % 2], 32 * (t // 2 + 1))
                    if t:
                        pe.wait_ge(a["ke"], 3 * t)
                    for g, n in enumerate((4, 4, 2)):
                        for j in range(n):
                            at = QB + (t % 2) * NKH * HD + (4 * g + j) * HD
                            ins = nc.tensor.transpose(bank(4 + g, 512)[:, j * P:(j + 1) * P], bg(at, HD), ident[:, :])
                        ins.then_inc(a["kt"], 1)
                pe.wait_ge(a["ke"], 3 * T)
                pe.wait_ge(a["v"], 32 * T + (16 if s == 0 else 0))

                with pe.Fori(0, blocks) as i:
                    qb = i + s * SB
                    def scores(sc):
                        kh = sc // 4 if sc < 8 else KVH + sc - 8
                        pe.wait_ge(a["ex"], qb * 16 + sc + 1)
                        lo = (sc % 2) * 1024
                        for c0 in range(0, T * P, 512):
                            n = min(512, T * P - c0)
                            ins = nc.tensor.matmul(ps[:, lo + c0:lo + c0 + n], qT[:, sc], kT[:, kh, c0:c0 + n], start=True, stop=True)
                        ins.then_inc(a["sc"], 1)

                    def turn_weights(o, sc):
                        pe.wait_ge(a["pn"], qb * 12 + o + 1)
                        if o:
                            pe.wait_ge(a["pe"], qb * 12 + o)
                        for t in range(T):
                            ins = nc.tensor.transpose(ps[:, 2048 + t * P:2048 + (t + 1) * P],
                                                      zt_f[:, (sc % 4) * 640 + t * P:(sc % 4) * 640 + (t + 1) * P], ident[:, :])
                        ins.then_inc(a["pt"], 1)

                    def output(o):
                        pe.wait_ge(a["pe"], qb * 12 + o + 1)
                        if o >= 2:
                            pe.wait_ge(a["oe"], qb * 12 + o + 1)
                        v0, vn = ((o // 4) * HD, HD) if o < 8 else (KVH * HD + (o - 8) * VD, VD)
                        for t in range(T):
                            ins = nc.tensor.matmul(bank(6 + o % 2, vn), ac(PTB + (o % 2) * 640 + t * P, P), bg(VB + t * VW + v0, vn),
                                                   start=(t == 0), stop=(t == T - 1))
                        ins.then_inc(a["pv"], 1)

                    pe.wait_ge(a["q"], qb * 32 + 32)
                    pe.wait_ge(a["oe"], qb * 12 + 2)
                    for g in range(4):
                        for j in range(4):
                            ins = nc.tensor.transpose(bank(4 + g, 512)[:, j * P:(j + 1) * P], bg(QB + (4 * g + j) * HD, HD), ident[:, :])
                        ins.then_inc(a["qt"], 1)
                    pe.wait_ge(a["qe"], qb * 4 + 4)
                    scores(0)
                    scores(1)
                    for sc in range(16):
                        if sc + 2 < 16:
                            scores(sc + 2)
                        o = done_output(sc)
                        if o is not None:
                            turn_weights(o, sc)
                            if o:
                                output(o - 1)
                    output(11)

            pe.wait_ge(att[1]["oe"], 12 * NB + 2)
            pe.wait_ge(sk_in, 16)
            for g in range(4):
                for j in range(4):
                    ins = nc.tensor.transpose(bank(4 + g)[:, j * P:(j + 1) * P], hcur[:, (4 * g + j) * HD:(4 * g + j + 1) * HD], ident[:, :])
                ins.then_inc(sk_t, 1)
            pe.wait_ge(sk_e, 4)

            for g in range(2):
                n, G = GROUP[g], grp[g]

                def bk(v):
                    return v % 4

                for lb in range(n):
                    pe.wait_ge(G["nat"][lb % 2], 16 * (lb // 2 + 1))
                    transposes(T_O[g] + lb, zn((lb % 2) * D, D))
                pe.wait_ge(t_free, (T_O[g] + n) * 4 + 4)
                with pe.Fori(0, DCH) as c:
                    u = c * (4 * n) + U_BR[g]
                    for p_ in range(2):
                        chunk(hT[g], H_BR[g] + 2 * p_, c, 6, n, u + p_ * n, lambda b: bk(p_ * n + b), 4)
                    for p_ in range(2):
                        nh = H_BR[g] + 4 + p_
                        wait_half(nh, c, 6)
                        for b in range(n):
                            v = (2 + p_) * n + b
                            pe.wait_ge(bank_free, u + (v + 2))
                            products(oT[g][:, p_ * (KT // 2):(p_ + 1) * (KT // 2)], b, nh, bk(v), True, True).then_inc(mm_done, 1)
                        release(u + (3 + p_) * n)
                for lb in range(n):
                    first = (n + 1 - lb % 2) // 2
                    pe.wait_ge(G["nat"][lb % 2], 16 * (first + lb // 2 + 1))
                    transposes(T_M[g] + lb, zn((lb % 2) * D, D))
                pe.wait_ge(t_free, (T_M[g] + n) * 4 + 4)
                for c in range(DCH):
                    chunk(mT[g], H_OUT[g] + 2 * c, 0, 0, n, U_OUT[g] + c * n, lambda b: bk(c * n + b), 4)
                for lb in range(n):
                    pe.wait_ge(nrm[g]["h"], lb + 1)
                    transposes(T_H[g] + lb, nbuf[g][1])
                pe.wait_ge(t_free, (T_H[g] + n) * 4 + 4)

                units = DCH * n

                def turn(v):
                    pe.wait_ge(bank_free, U_QRY[g] + v + NB + 1)
                    if v:
                        pe.wait_ge(G["te"], v)
                    for q in range(4):
                        ins = nc.tensor.transpose(bank(5)[:, q * P:(q + 1) * P], zt[:, v % 4, q * P:(q + 1) * P], ident[:, :])
                    ins.then_inc(G["tq"], 1)

                def keys(v):
                    pe.wait_ge(G["te"], v + 1)
                    if v:
                        pe.wait_ge(G["se"], v)
                    for q in range(4):
                        at = (4 * (v // n) + q) * P
                        ins = nc.tensor.matmul(bank(6)[:, q * P:(q + 1) * P], qts[:, q * P:(q + 1) * P], misc[:, at:at + P], start=True, stop=True)
                    ins.then_inc(G["sk"], 1)

                for c in range(DCH):
                    nh = H_QRY[g] + 2 * c
                    for h in range(2):
                        wait_half(nh + h, 0, 0)
                        for b in range(n):
                            v = c * n + b
                            if h == 0:
                                pe.wait_ge(bank_free, U_QRY[g] + v + 2)
                            ins = products(h2T[g][:, h * (KT // 2):(h + 1) * (KT // 2)], b, nh + h, bk(v), h == 0, h == 1)
                            if h == 1:
                                ins.then_inc(mm_done, 1)
                                if v >= 1:
                                    turn(v - 1)
                                if v >= 2:
                                    keys(v - 2)
                        if h == 0:
                            ins.then_inc(w_free, 1)
                    release(U_QRY[g] + (c + 1) * n)
                turn(units - 1)
                keys(units - 2)
                keys(units - 1)

        @block.scalar
        def _(sa):
            def evac(u, bk, to, func=ACT.Copy):
                sa.wait_ge(mm_done, u + 1)
                nc.scalar.activation(to, bank(bk), func).then_inc(bank_free, 1)

            def transposed(B, b, dst):
                for q in range(4):
                    sa.wait_ge(t_done, B * 4 + q + 1)
                    nc.scalar.activation(dst[:, 4 * q:4 * q + 4, b * P:(b + 1) * P],
                                         bank(4 + q).rearrange("p (k n) -> p k n", k=4), ACT.Copy).then_inc(t_free, 1)

            def root(s, b):
                sa.wait_ge(nrm_ms, s["base"] + b + 1)
                nc.scalar.activation(small[:, 1:2], small[:, 0:1], ACT.Sqrt).then_inc(nrm_rs, 1)

            def top_exps(step):
                sa.wait_ge(tk_neg, step + 1)
                nc.scalar.activation(ex16, top, ACT.Exp, bias=ntop, accum_out=exsum).then_inc(tk_exp, 1)

            def gelus(g, at):
                sa.wait_ge(ring_free[g], at + RINGS[g] + TOPK)
                nc.scalar.activation(gel, dots, ACT.Gelu).then_inc(ge_done, 1)

            sa.sem_inc(bank_free, NB)
            sa.sem_inc(t_free, 4)
            sa.sem_inc(att[0]["ex"], 2)
            sa.wait_ge(cond_in, 32)
            nc.scalar.activation(small[:, 32:64], small[:, 0:32], ACT.Sigmoid).then_inc(cond_sig, 1)
            sa.wait_ge(lam_dot, 1)
            nc.scalar.activation(small[:, 4:6], small[:, 4:6], ACT.Exp).then_inc(lam_exp, 1)
            for b in range(NB):
                root(nrm[2], b)
                transposed(b, b % SB, hT[1] if b < SB else hT[0])

            def qkv_unit(u, b, normed):
                sa.wait_ge(zo_ready, u + 1)
                evac(u, b, zt[:, b])
                if normed:
                    sa.wait_ge(qn_ms, u + 1)
                    nc.scalar.activation(small[:, 12:16], small[:, 8:12], ACT.Sqrt).then_inc(qn_rs, 1)
            with sa.Fori(0, 3) as r:
                for b in range(NB):
                    qkv_unit(r * NB + b, b, True)
            with sa.Fori(0, QKV_CH - 3) as r:
                for b in range(NB):
                    qkv_unit(r * NB + 3 * NB + b, b, False)

            for s in range(2):
                a = att[s]
                T, blocks = (SB + 1, SB) if s == 0 else (1, 1)
                kT = ac(KTB, NKH * T * P).rearrange("p (h n) -> p h n", h=NKH)
                for t in range(T):
                    for g, n in enumerate((4, 4, 2)):
                        sa.wait_ge(a["kt"], 3 * t + g + 1)
                        nc.scalar.activation(kT[:, 4 * g:4 * g + n, t * P:(t + 1) * P],
                                             bank(4 + g, n * P).rearrange("p (h n) -> p h n", h=n), ACT.Copy).then_inc(a["ke"], 1)
                with sa.Fori(0, blocks) as i:
                    qb = i + s * SB
                    def exps(sc):
                        if sc < 4:
                            last = 8 + (sc + 4) // 2
                            sa.wait_ge(a["pt"], qb * 12 + last + 1)
                        else:
                            last = sc - 4 if sc - 4 < 8 else 8 + (sc - 12) // 2
                            sa.wait_ge(a["pt"], qb * 12 + 12 + last + 1)
                        sa.wait_ge(a["nm"], qb * 16 + sc + 1)
                        lo, sl = (sc % 2) * 1024, sc % 4
                        nc.scalar.activation(zt_f[:, sl * 640:sl * 640 + T * P], ps[:, lo:lo + T * P], ACT.Exp,
                                             bias=small[:, 16 + sl:17 + sl], scale=SCALE,
                                             accum_out=small[:, 20 + sl:21 + sl]).then_inc(a["ex"], 1)

                    for g in range(4):
                        sa.wait_ge(a["qt"], qb * 4 + g + 1)
                        nc.scalar.activation(misc[:, g * 512:(g + 1) * 512], bank(4 + g), ACT.Copy).then_inc(a["qe"], 1)
                    exps(0)
                    exps(1)
                    for sc in range(16):
                        o = done_output(sc)
                        if o is not None:
                            sa.wait_ge(a["pt"], qb * 12 + 12 + o + 1)
                            sa.wait_ge(a["pv"], qb * 12 + o + 1)
                            nc.scalar.activation(ac(PTB + (o % 2) * 640, T * P), ps[:, 2048:2048 + T * P], ACT.Copy).then_inc(a["pe"], 1)
                        if sc + 2 < 16:
                            exps(sc + 2)
                    sa.wait_ge(a["ms"], qb + 1)
                    nc.scalar.activation(small[:, 12:16], small[:, 8:12], ACT.Sqrt).then_inc(a["rs"], 1)

            for g in range(4):
                sa.wait_ge(sk_t, g + 1)
                nc.scalar.activation(misc[:, g * 512:(g + 1) * 512], bank(4 + g), ACT.Copy).then_inc(sk_e, 1)

            for g in range(2):
                n, G = GROUP[g], grp[g]
                for lb in range(n):
                    transposed(T_O[g] + lb, lb, oT[g])
                with sa.Fori(0, DCH) as c:
                    u = c * (4 * n) + U_BR[g]
                    for p_ in range(2):
                        for lb in range(n):
                            if p_ == 0:
                                sa.wait_ge(G["gates"], c * n + lb + 1)
                            v = p_ * n + lb
                            evac(u + v, v % 4, zn((p_ * SB + lb) * CH, CH), ACT.Sigmoid)
                        if g and p_ == 0:
                            top_exps(c + 1)
                            gelus(0, c * (2 * TOPK))
                    for p_ in range(2):
                        for lb in range(n):
                            v = (2 + p_) * n + lb
                            sa.wait_ge(G["zt"], c * (2 * n) + p_ * n + lb + 1)
                            evac(u + v, v % 4, zt[:, v % 4])
                for lb in range(n):
                    transposed(T_M[g] + lb, lb, mT[g])
                for c in range(DCH):
                    for lb in range(n):
                        v = c * n + lb
                        if v == 0:
                            sa.wait_ge(G["zt"], 2 * n * DCH + (4 if g else 2))
                        if v >= 4:
                            sa.wait_ge(G["ou_st"][v % 4], 16 * (v // 4))
                        evac(U_OUT[g] + v, v % 4, zt[:, v % 4])
                    if g and c in (0, 2):
                        step = 4 + c // 2
                        top_exps(step + 1)
                        gelus(0, step * 2 * TOPK)
                for lb in range(n):
                    root(nrm[g], lb)
                    transposed(T_H[g] + lb, lb, h2T[g])
                units = DCH * n
                for v in range(units + 2):
                    if v < units:
                        if v >= 4:
                            sa.wait_ge(G["tq"], v - 3)
                        evac(U_QRY[g] + v, v % 4, zt[:, v % 4])
                    if 1 <= v <= units:
                        sa.wait_ge(G["tq"], v)
                        if v >= 2:
                            sa.wait_ge(G["sk"], v - 1)
                        nc.scalar.activation(qts[:, :], bank(5), ACT.Copy).then_inc(G["te"], 1)
                    if v >= 2:
                        x = v - 2
                        sa.wait_ge(G["sk"], x + 1)
                        if x >= 4:
                            sa.wait_ge(G["sc_st"][x % 4], 16 * (x // 4))
                        nc.scalar.activation(zn((x % 4) * CH, CH), bank(6), ACT.Copy).then_inc(G["se"], 1)
                    if g and v in (3, 9):
                        step = 6 if v == 3 else 7
                        if step < 7:
                            top_exps(step + 1)
                        gelus(0, step * 2 * TOPK)
                if g == 0:
                    top_exps(0)
            top_exps(PH)
            sa.wait_ge(f_ms, 1)
            nc.scalar.activation(small[:, 1:2], small[:, 0:1], ACT.Sqrt).then_inc(f_rs, 1)
            with sa.Fori(0, SB) as b:
                with sa.Fori(0, PH) as h:
                    m = b * PH + h
                    top_exps(m + PH + 1)
                    gelus(1, m * (2 * TOPK))
                sa.wait_ge(f_ms, b + 2)
                nc.scalar.activation(small[:, 1:2], small[:, 0:1], ACT.Sqrt).then_inc(f_rs, 1)

        @block.vector
        def _(dve):
            ch = Chain(dve, dve_s)
            link = ch.link
            V = nc.vector

            def signal(ins, s, value):
                ins.then_inc(s, 1)
                dve.wait_ge(s, value)

            for s_, n in ((ada_free, 3), (zo_ready, NB), (grp[0]["gates"], GROUP[0]), (grp[1]["gates"], GROUP[1]), (grp[0]["zt"], 2),
                          (grp[1]["zt"], 4), (att[0]["pt"], 12), (att[0]["oe"], 2)):
                dve.sem_inc(s_, n)
            dve.wait_ge(cond_sig, 1)
            signal(V.tensor_tensor(small[:, 64:96].rearrange("p (t c) -> p c t", c=2), small[:, 0:32].rearrange("p (c t) -> p c t", c=2),
                                   small[:, 32:64].rearrange("p (c t) -> p c t", c=2), ALU.mult), cond_ready, 1)
            dve.wait_ge(lam_in, 64)
            for n in range(2):
                link(V.tensor_tensor_reduce(out=misc[:, 512:512 + HD], in0=misc[:, 2 * n * HD:(2 * n + 1) * HD],
                                            in1=misc[:, (2 * n + 1) * HD:(2 * n + 2) * HD], scale=1.0, scalar=0.0,
                                            op0=ALU.mult, op1=ALU.add, accum_out=small[:, 4 + n:5 + n]))
            dve.sem_inc(lam_dot, 1)
            dve.wait_ge(lam_exp, 1)
            link(V.tensor_tensor(small[:, 6:7], small[:, 5:6], small[:, 4:5], ALU.subtract))
            link(V.tensor_scalar(small[:, 6:7], small[:, 6:7], -LAM_INIT, None, ALU.add))
            dve.wait_ge(bada_in, 16)
            with dve.Fori(0, ADA_CH // 3) as i:
                for j in range(3):
                    dve.wait_ge(ada_mm, i * 3 + j + 1)
                    dve.nop(nofuse=True)
                    V.tensor_tensor(zt[0:2, j], ps[0:2, j * 512:(j + 1) * 512], act[0:2, ds(i * (3 * CH) + j * CH, CH)],
                                    ALU.add).then_inc(ada_free, 1)
                for j in range(3):
                    dve.wait_ge(ada_out[j], i * 16 + 16)
            dve.wait_ge(ada_free, 3 + ADA_CH)

            def norm(s, g, blocks, T0):
                xb, h, A, Bv, gain = nbuf[g]
                for b in range(blocks):
                    x = xb[b % 2]
                    if b in (0, SB):
                        dve.wait_ge(s["row"], 48 if b == 0 else 80)
                        link(V.scalar_tensor_tensor(A, A, 1.0, gain, ALU.add, ALU.mult))
                    dve.wait_ge(s["x"][b % 2], 16 * (b // 2 + 1))
                    if b:
                        dve.wait_ge(t_done, 4 * (T0 + b))
                        if s is nrm[1]:
                            dve.wait_ge(h2_out, 16 * b)
                    link(V.tensor_tensor_reduce(out=h, in0=x, in1=x, scale=1.0, scalar=0.0, op0=ALU.mult, op1=ALU.add,
                                                accum_out=small[:, 2:3]))
                    signal(V.tensor_scalar(small[:, 0:1], small[:, 2:3], 1.0 / D, EPS, ALU.mult, ALU.add), nrm_ms, s["base"] + b + 1)
                    dve.wait_ge(nrm_rs, s["base"] + b + 1)
                    link(V.reciprocal(small[:, 3:4], small[:, 1:2]))
                    link(V.scalar_tensor_tensor(h, x, small[:, 3:4], A, ALU.mult, ALU.mult))
                    signal(V.tensor_tensor(h, h, Bv, ALU.add), s["h"], b + 1)

            norm(nrm[2], 1, NB, 0)

            def zo(b):
                return ac(QZ + b * CH, CH)
            t1, t2 = ac(QZ + NB * CH, CH), ac(QZ + (NB + 1) * CH, CH)
            qgain, kgain = ac(QT + 2 * SB * HD, HD), ac(QT + 2 * SB * HD + HD, HD)

            def hview(ap, h):
                return ap.rearrange("p (h d) -> p h d", h=h)

            def halves(ap, h):
                return ap.rearrange("p (h a e d) -> p h a e d", h=h, a=2, e=2)

            def head_norm(u, b, nh, g):
                z = zt[:, b, 0:nh * HD]
                link(V.tensor_tensor(t1[:, 0:nh * HD], z, z, ALU.mult))
                link(V.tensor_reduce(small[:, 28:28 + nh], hview(t1[:, 0:nh * HD], nh), AX.X, ALU.add))
                signal(V.tensor_scalar(small[:, 8:8 + 4], small[:, 28:32], 1.0 / HD, EPS, ALU.mult, ALU.add), qn_ms, u + 1)
                dve.wait_ge(qn_rs, u + 1)
                link(V.reciprocal(small[:, 24:28], small[:, 12:16]))
                link(V.tensor_tensor(hview(z, nh), hview(z, nh), small[:, 24:24 + nh].unsqueeze(2).to_broadcast([P, nh, HD]), ALU.mult))
                link(V.tensor_tensor(hview(z, nh), hview(z, nh), g.unsqueeze(1).to_broadcast([P, nh, HD]), ALU.mult))

            def finish(u, b, nh):
                rot = nh if b < SB else 0
                if rot:
                    cos = ac(QT + b * HD, HD)
                    sin = ac(QT + SB * HD + b * HD, HD).rearrange("p (a e d) -> p a e d", a=2, e=2)
                    z, n = zt[:, b, 0:rot * HD], rot * HD
                    link(V.tensor_tensor(hview(t1[:, 0:n], rot), hview(z, rot), cos.unsqueeze(1).to_broadcast([P, rot, HD]), ALU.mult))
                    for e in range(2):
                        link(V.tensor_tensor(halves(t2[:, 0:n], rot)[:, :, :, e], halves(z, rot)[:, :, :, 1 - e],
                                             sin[:, :, e].unsqueeze(1).to_broadcast([P, rot, 2, HD // 4]), ALU.mult))
                    if rot < 4:
                        link(V.tensor_copy(zo(b)[:, n:CH], zt[:, b, n:CH]))
                    ins = V.tensor_tensor(zo(b)[:, 0:n], t1[:, 0:n], t2[:, 0:n], ALU.add)
                else:
                    ins = V.tensor_copy(zo(b), zt[:, b])
                signal(ins, zo_ready, u + NB + 1)

            def stored(sems, count):
                for s_ in sems:
                    dve.wait_ge(s_, count)

            dve.wait_ge(qk_tab, 64)
            link(V.memset(small[:, 28:32], 0.0))
            with ch.loop(2, 5 * NB + 3 * SB) as r:
                for b in range(NB):
                    dve.wait_ge(bank_free, r * NB + b + NB + 1)
                    head_norm(r * NB + b, b, 4, qgain)
                    finish(r * NB + b, b, 4)
                stored(zo_out, r * 16 + 16)
            for b in range(NB):
                dve.wait_ge(bank_free, 2 * NB + b + NB + 1)
                head_norm(2 * NB + b, b, 2, kgain)
                finish(2 * NB + b, b, 2)
            stored(zo_out, 48)
            with ch.loop(4, 3 * SB) as r:
                for b in range(NB):
                    dve.wait_ge(bank_free, r * NB + 3 * NB + b + NB + 1)
                    finish(r * NB + 3 * NB + b, b, 4)
                stored(zo_out, r * 16 + 64)
            with ch.loop(2, 0) as r:
                for b in range(NB):
                    dve.wait_ge(bank_free, r * NB + 7 * NB + b + NB + 1)
                    finish(r * NB + 7 * NB + b, b, 0)
                stored(zo_out, r * 16 + 128)

            for s in range(2):
                a = att[s]
                T, blocks = (SB + 1, SB) if s == 0 else (1, 1)

                def weights(sc):
                    return zt_f[:, (sc % 4) * 640:(sc % 4) * 640 + T * P]

                with ch.loop(blocks, 16 + 16 + 2 * DH + 5) as i:
                    qb = i + s * SB
                    def maxes(sc):
                        dve.wait_ge(a["sc"], qb * 16 + sc + 1)
                        lo = (sc % 2) * 1024
                        link(V.tensor_reduce(small[:, 32 + sc % 4:33 + sc % 4], ps[:, lo:lo + T * P], AX.X, ALU.max))
                        signal(V.tensor_scalar(small[:, 16 + sc % 4:17 + sc % 4], small[:, 32 + sc % 4:33 + sc % 4], -SCALE, None, ALU.mult),
                               a["nm"], qb * 16 + sc + 1)

                    def normed(sc):
                        inv = small[:, 36 + sc % 4:37 + sc % 4]
                        dve.wait_ge(a["ex"], qb * 16 + sc + 3)
                        link(V.reciprocal(inv, small[:, 20 + sc % 4:21 + sc % 4]))
                        if sc < 8:
                            V.tensor_scalar(weights(sc), weights(sc), inv, None, ALU.mult).then_inc(a["pn"], 1)
                        elif sc % 2 == 0:
                            link(V.tensor_scalar(weights(sc), weights(sc), inv, None, ALU.mult))
                        else:
                            link(V.tensor_scalar(inv, inv, small[:, 6:7], None, ALU.mult))
                            V.scalar_tensor_tensor(weights(sc), weights(sc), inv, weights(sc - 1), ALU.mult, ALU.add).then_inc(a["pn"], 1)

                    def out(o):
                        dve.wait_ge(a["pv"], qb * 12 + o + 3)
                        c0, n = (o * HD, HD) if o < 8 else (QH * HD + (o - 8) * VD, VD)
                        V.tensor_copy(onat[:, c0:c0 + n], bank(6 + o % 2, n)).then_inc(a["oe"], 1)

                    maxes(0)
                    maxes(1)
                    for sc in range(16):
                        normed(sc)
                        if sc + 2 < 16:
                            maxes(sc + 2)
                        o = done_output(sc)
                        if o is not None and o >= 2:
                            out(o - 2)
                    out(10)
                    out(11)
                    dve.wait_ge(a["oe"], qb * 12 + 14)
                    od = onat[:, QH * HD:D]
                    link(V.tensor_tensor(tmp4, od, od, ALU.mult))
                    link(V.tensor_reduce(small[:, 28:32], hview(tmp4, DH), AX.X, ALU.add))
                    signal(V.tensor_scalar(small[:, 8:12], small[:, 28:32], 1.0 / VD, EPS, ALU.mult, ALU.add), a["ms"], qb + 1)
                    dve.wait_ge(a["rs"], qb + 1)
                    link(V.reciprocal(small[:, 24:28], small[:, 12:16]))
                    link(V.tensor_scalar(small[:, 24:28], small[:, 24:28], 1.0 - LAM_INIT, None, ALU.mult))
                    link(V.tensor_tensor(hview(od, DH), hview(od, DH), small[:, 24:28].unsqueeze(2).to_broadcast([P, DH, VD]), ALU.mult))
                    signal(V.tensor_tensor(hview(od, DH), hview(od, DH), subg.unsqueeze(1).to_broadcast([P, DH, VD]), ALU.mult),
                           a["o"], qb + 1)
                    dve.wait_ge(a["st"], qb * 16 + 16)

            def pick(src, spare, v16, i16):
                for half in range(2):
                    s_ = src if half == 0 else spare
                    v8, i8 = v16[:, 8 * half:8 * half + 8], i16[:, 8 * half:8 * half + 8]
                    dve.nop(nofuse=True)
                    link(V.max(out=v8, in_=s_))
                    dve.nop(nofuse=True)
                    link(V.max_index(out=i8, in_max=v8, in_values=s_))
                    if half == 0:
                        dve.nop(nofuse=True)
                        link(V.match_replace(out=spare, in_to_replace=v8, in_values=src, imm_value=NEG))

            def choose(step, q):
                dve.wait_ge(sc_in, step * 16 + 16)
                for c in range(2):
                    pick(sc2[:, c * NK:(c + 1) * NK], rep[:, c * NK:(c + 1) * NK], vals[:, c * 16:c * 16 + 16], valsi[:, c * 16:c * 16 + 16])
                link(V.tensor_tensor(cand.rearrange("p (i j) -> p i j", i=TOPK), vals[:, 0:16].unsqueeze(2).to_broadcast([P, TOPK, TOPK]),
                                     vals[:, 16:32].unsqueeze(1).to_broadcast([P, TOPK, TOPK]), ALU.add))
                pick(cand, cand2, top, candi)
                V.tensor_scalar(ntop, top[:, 0:1], -1.0, None, ALU.mult).then_inc(tk_neg, 1)
                link(V.tensor_scalar(hl[:, 0:16], candi, 4, None, ALU.logical_shift_right))
                link(V.tensor_scalar(hl[:, 16:32], candi, 15, None, ALU.bitwise_and))
                link(V.tensor_copy(hlf, hl))
                link(V.tensor_copy(vif, valsi))
                o4 = oh.rearrange("p (c w j) -> p c w j", c=2, w=TOPK)
                for c in range(2):
                    link(V.tensor_tensor(o4[:, c], hlf[:, c * 16:c * 16 + 16].unsqueeze(2).to_broadcast([P, TOPK, TOPK]),
                                         iota16[:, :].unsqueeze(1).to_broadcast([P, TOPK, TOPK]), ALU.is_equal))
                    link(V.tensor_tensor(o4[:, c], o4[:, c], vif[:, c * 16:c * 16 + 16].unsqueeze(1).to_broadcast([P, TOPK, TOPK]), ALU.mult))
                link(V.tensor_reduce(eidx, oh.rearrange("p (w j) -> p w j", j=TOPK), AX.X, ALU.add))
                link(V.scalar_tensor_tensor(sel[:, q], eidx[:, 0:16], float(NK), eidx[:, 16:32], ALU.mult, ALU.add))
                dve.wait_ge(tk_exp, step + 1)
                link(V.reciprocal(rsum, exsum))
                signal(V.tensor_scalar(wts[:, q * 16:q * 16 + 16], ex16, rsum, None, ALU.mult), sel_ready, step + 1)

            CHOOSE = 5 * 3 + 1 + 4 + 4 + 2 + 1
            STEP = CHOOSE + 1

            def peer_step(g, step, q, m, ahead=True):
                R = RINGS[g]
                for k in range(TOPK):
                    dve.wait_ge(ring_in[g][k % R], m * (32 // R * 16) + (k // R + 1) * 16)
                    t = slot(g, k)
                    V.tensor_tensor_reduce(out=t, in0=t, in1=hcur, scale=1.0, scalar=0.0, op0=ALU.mult, op1=ALU.add,
                                           accum_out=dots[:, k:k + 1]).then_inc(ring_free[g], 1)
                if ahead:
                    choose(step + 1, 1 - q)
                dve.wait_ge(ge_done, step + 1)
                link(V.tensor_tensor(coef, gel, wts[:, q * 16:q * 16 + 16], ALU.mult))
                for k in range(TOPK):
                    dve.wait_ge(ring_in[g][k % R], m * (32 // R * 16) + ((TOPK + k) // R + 1) * 16)
                    signal(V.scalar_tensor_tensor(acc, slot(g, k), coef[:, k:k + 1], acc, ALU.mult, ALU.add),
                           ring_free[g], m * 32 + R + TOPK + k + 1)

            def final(x1, gate, gain, nth):
                link(V.tensor_tensor(acc, acc, gate, ALU.mult))
                link(V.tensor_tensor(acc, acc, x1, ALU.add))
                link(V.tensor_tensor_reduce(out=x1, in0=acc, in1=acc, scale=1.0, scalar=0.0, op0=ALU.mult, op1=ALU.add,
                                            accum_out=small[:, 2:3]))
                signal(V.tensor_scalar(small[:, 0:1], small[:, 2:3], 1.0 / D, EPS, ALU.mult, ALU.add), f_ms, nth)
                dve.wait_ge(f_rs, nth)
                link(V.reciprocal(small[:, 3:4], small[:, 1:2]))
                link(V.scalar_tensor_tensor(x1, acc, small[:, 3:4], gain, ALU.mult, ALU.mult))
                dve.sem_inc(y_ready, 1)

            for g in range(2):
                n, G = GROUP[g], grp[g]

                def merge(c):
                    u = c * (4 * n) + U_BR[g]
                    for lb in range(n):
                        dve.wait_ge(bank_free, u + (2 * n + lb + NB + 1))
                        link(V.tensor_tensor(zn(lb * CH, CH), zn(lb * CH, CH), zt[:, (2 * n + lb) % 4], ALU.mult))
                        dve.sem_inc(G["zt"], 1)
                    for lb in range(n):
                        gb = zn((SB + lb) * CH, CH)
                        dve.wait_ge(bank_free, u + (3 * n + lb + NB + 1))
                        link(V.tensor_tensor(gb, gb, zt[:, (3 * n + lb) % 4], ALU.mult))
                        dve.sem_inc(G["zt"], 1)
                        signal(V.tensor_tensor(zn(lb * CH, CH), zn(lb * CH, CH), gb, ALU.add), G["br"], c * n + lb + 1)
                    stored(G["br_st"], c * 16 + 16)
                    dve.sem_inc(G["gates"], n)

                def residual(c):
                    for lb in range(n):
                        v = c * n + lb
                        dve.wait_ge(bank_free, U_OUT[g] + v + NB + 1)
                        link(V.tensor_tensor(zt[:, v % 4], zt[:, v % 4], zn(c * CH, CH), ALU.mult))
                        dve.wait_ge(G["xt"][lb], 16 * (c + 1))
                        signal(V.tensor_tensor(zt[:, v % 4], zt[:, v % 4], zn(D + lb * CH, CH), ALU.add), G["ou"], v + 1)

                if g == 0:
                    with ch.loop(DCH, 2 * n) as c:
                        merge(c)
                else:
                    with ch.loop(DCH // 2, 2 * (STEP + 2 * n)) as i:
                        for j in range(2):
                            peer_step(0, i * 2 + j, j, i * 2 + j)
                            merge(i * 2 + j)
                dve.wait_ge(G["g1"], 16)
                for c in range(DCH):
                    residual(c)
                    if g and c in (0, 2):
                        peer_step(0, 4 + c // 2, c // 2, 4 + c // 2)
                norm(nrm[g], g, n, T_H[g])
                if g == 0:
                    link(V.memset(acc, 0.0))
                    choose(0, 0)
                    dve.sem_inc(ring_free[0], RINGS[0])
                else:
                    for j in range(2):
                        peer_step(0, 6 + j, j, 6 + j, ahead=j == 0)

            choose(PH, 0)
            dve.wait_ge(grp[1]["sk"], DCH * SB)
            dve.sem_inc(ring_free[1], RINGS[1])
            dve.wait_ge(fa_in, 48)
            final(ac(A1, D), ac(A1 + D, D), ac(A1 + 2 * D, D), 1)
            start = ch.base + ch.k
            per_block = PH * STEP + 2 + 5
            with dve.Fori(0, SB) as b:
                ch.base, ch.k = b * per_block + start, 0
                dve.wait_ge(hn_in, b * 16 + 16)
                link(V.tensor_copy(hcur, ac(2 * D, D)))
                dve.sem_inc(h_taken, 1)
                link(V.memset(acc, 0.0))
                dve.nop(nofuse=True)
                with dve.Fori(0, PH // 2) as hp:
                    for q in range(2):
                        ch.base, ch.k = b * per_block + start + 2 + hp * (2 * STEP) + q * STEP, 0
                        m = b * PH + hp * 2 + q
                        peer_step(1, m + PH, q, m)
                        assert ch.k == STEP
                ch.base, ch.k = b * per_block + start + 2 + PH * STEP, 0
                dve.wait_ge(fx_in, b * 16 + 32)
                final(ac(0, D), ac(D, D), ac(A1 + 2 * D, D), b + 2)
                assert ch.k == 5


_INS = ["x_prompt", "x_sample", "c", "cache_gqa_k", "cache_gqa_v", "cache_diff_k", "cache_diff_v", "c_ctx", "w_ada", "b_ada",
        "norm1_g", "norm2_g", "w_in", "q_norm_g", "k_norm_g", "lambda_q1", "lambda_k1", "lambda_q2", "lambda_k2",
        "diff_subln_g", "w_branch_a", "w_branch_b", "w_out", "peer_w_query", "peer_sub_keys", "peer_u", "peer_v",
        "final_norm_g"]
_OUTS = [(1, SEQ, D), (1, DEC_SEQ, D), (1, 1, SEQ, KVH, HD), (1, 1, SEQ, KVH, HD), (1, 1, SEQ, DH, 2, HD), (1, 1, SEQ, DH, VD)]


def rope_tables():
    f = np.float32
    rows = DEC_SEQ // GRID_W
    row = np.repeat(np.arange(rows, dtype=f), GRID_W)
    col = np.tile(np.arange(GRID_W, dtype=f), rows)
    pairs = HD // 4
    inv = np.power(f(10000.0), -np.arange(pairs, dtype=f) / f(pairs)).astype(f)
    ar, ac = row[:, None] * inv, col[:, None] * inv
    ang = np.concatenate([ar, ar, ac, ac], axis=-1)
    sign = np.repeat(np.array([-1, 1, -1, 1], f), pairs)
    return np.cos(ang).astype(f), (np.sin(ang) * sign).astype(f)


def kernel(**inputs):
    import concourse.bacc as bacc
    from concourse.bass_utils import run_bass_kernel_spmd

    nc = bacc.Bacc("TRN2", target_bir_lowering=False, num_devices=1)
    arrays, I = {}, {}
    cos, sin = rope_tables()
    for name, a in [(n, np.ascontiguousarray(inputs[n])) for n in _INS] + [("rope_cos", cos), ("rope_sin", sin)]:
        arrays[f"in_{name}"] = a
        I[name] = nc.dram_tensor(f"in_{name}", a.shape, mybir.dt.from_np(a.dtype), kind="ExternalInput").ap()
    O = [nc.dram_tensor(f"out_{i}", s, mybir.dt.float32, kind="ExternalOutput").ap() for i, s in enumerate(_OUTS)]
    build(nc, I, O)
    r = run_bass_kernel_spmd(nc, [arrays], core_ids=[0])
    return tuple(r.results[0][f"out_{i}"] for i in range(len(_OUTS)))
```

```python
import math
from contextlib import ExitStack, contextmanager

import numpy as np

import concourse.bass as bass
from concourse import mybir

D = 2048
SEQ = 128
DEC_SEQ = 512
PAST = 128
GRID_W = 64
HD = 128
QH, KVH, DH = 8, 2, 4
VD = 2 * HD
P = 128
KT = D // P
NB = (SEQ + DEC_SEQ) // P
SB = DEC_SEQ // P
CH = 512
PROJ_W = QH * HD + 2 * KVH * HD + 2 * DH * 2 * HD + DH * VD + 2 * D
QG0, KG0, VG0 = 0, QH * HD, (QH + KVH) * HD
QD0 = (QH + 2 * KVH) * HD
KD0 = QD0 + 2 * DH * HD
VD0 = KD0 + 2 * DH * HD
ZW = VD0 + DH * VD
NKH = KVH + 2 * DH
VW = KVH * HD + DH * VD
ADA_CH, QKV_CH, DCH = 6 * D // CH, ZW // CH, D // CH
GROUP = (1, 1, SB - 1)
ATT_BLOCKS = (1, SB)
WS = 3
HALF = KT // 2 * CH
QKV_HALVES, GROUP_HALVES = 2 * QKV_CH, 10 * DCH
H_QKV = (2 * ADA_CH, 2 * ADA_CH + QKV_HALVES + GROUP_HALVES)
H_BR = (H_QKV[0] + QKV_HALVES, H_QKV[1] + QKV_HALVES, H_QKV[1] + QKV_HALVES + GROUP_HALVES)
H_OUT = tuple(h + 6 * DCH for h in H_BR)
H_QRY = tuple(h + 2 * DCH for h in H_OUT)
U_QKV = (0, QKV_CH + 6 * DCH)
U_BR = (QKV_CH, U_QKV[1] + SB * QKV_CH, U_QKV[1] + SB * QKV_CH + 6 * DCH)
U_OUT = tuple(u + 4 * DCH * g for u, g in zip(U_BR, GROUP))
U_QRY = tuple(u + DCH * g for u, g in zip(U_OUT, GROUP))
T_O = (NB, NB + 3, NB + 6)
T_M = tuple(t + g for t, g in zip(T_O, GROUP))
T_H = tuple(t + g for t, g in zip(T_M, GROUP))
EPS = 1e-6
SCALE = HD ** -0.5
LAM_INIT = 0.8 - 0.6 * math.exp(-0.3 * 0)
NEG = -3.0e38
PH, NK, TOPK = 8, 128, 16
STEPS = NB * PH
RINGS = (4, 8)
STEP0 = (0, PH, 2 * PH)


class Chain:

    def __init__(self, eng, sem):
        self.eng, self.sem, self.base, self.k = eng, sem, 0, 0

    def link(self, ins):
        ins.then_inc(self.sem, 1)
        self.k += 1
        self.eng.wait_ge(self.sem, self.base + self.k)

    @contextmanager
    def loop(self, n, per):
        start = self.base + self.k
        with self.eng.Fori(0, n) as i:
            self.base, self.k = i * per + start, 0
            yield i
            assert self.k == per, self.k
        self.base, self.k = start + n * per, 0


def build(nc, I, O):
    f32, u32 = mybir.dt.float32, mybir.dt.uint32
    ALU, ACT, AX = mybir.AluOpType, mybir.ActivationFunctionType, mybir.AxisListType
    ds = bass.ds

    mod = nc.dram_tensor("mod_rows", (2, 6 * D), f32).ap()
    zs = nc.dram_tensor("z_blocks", (NB, P, ZW), f32).ap()
    osd = nc.dram_tensor("o_blocks", (NB, P, D), f32).ap()
    md = nc.dram_tensor("merged_blocks", (NB, P, D), f32).ap()
    x1d = nc.dram_tensor("x1_blocks", (NB, P, D), f32).ap()
    h2d = nc.dram_tensor("h2_blocks", (GROUP[2], P, D), f32).ap()
    scd = nc.dram_tensor("scores", (P, (STEPS + 1) * VD), f32).ap()

    xs = I["x_sample"].rearrange("a (b p) d -> (a b) p d", p=P)
    xp = I["x_prompt"].rearrange("a (b p) d -> (a b) p d", p=P)
    ys = O[1].rearrange("a (b p) d -> (a b) p d", p=P)
    yp = O[0].rearrange("a (b p) d -> (a b) p d", p=P)
    w_ada = I["w_ada"].rearrange("l (p t) n -> p (l t) n", p=P)
    w_in = I["w_in"].rearrange("l (t p) n -> p (l t) n", p=P)
    w_a = I["w_branch_a"].rearrange("l (t p) n -> p (l t) n", p=P)
    w_b = I["w_branch_b"].rearrange("l (t p) n -> p (l t) n", p=P)
    w_out = I["w_out"].rearrange("l (t p) n -> p (l t) n", p=P)
    w_qry = I["peer_w_query"].rearrange("l (t p) n -> p (l t) n", p=P)
    eu = I["peer_u"].rearrange("l e d -> (l e) d")
    ev = I["peer_v"].rearrange("l e d -> (l e) d")
    sub = I["peer_sub_keys"].rearrange("l h c k d -> k (l h c) d")
    ckg = I["cache_gqa_k"].rearrange("a l s h d -> (a l s) (h d)")
    cvg = I["cache_gqa_v"].rearrange("a l s h d -> (a l s) (h d)")
    ckd = I["cache_diff_k"].rearrange("a l s h c d -> (a l s) (h c d)")
    cvd = I["cache_diff_v"].rearrange("a l s h d -> (a l s) (h d)")
    nkg = O[2].rearrange("a l s h d -> (a l s) (h d)")
    nvg = O[3].rearrange("a l s h d -> (a l s) (h d)")
    nkd = O[4].rearrange("a l s h c d -> (a l s) (h c d)")
    nvd = O[5].rearrange("a l s h d -> (a l s) (h d)")

    ctx = ExitStack()
    with ctx:
        def sb(name, shape, dt=f32):
            return ctx.enter_context(nc.sbuf_tensor(name, shape, dt))

        def sem(name):
            return ctx.enter_context(nc.semaphore(name))

        act = sb("activations", [P, 2 * SB * D])
        big = sb("big", [P, WS * HALF + 6 * D])
        zone = sb("zone", [P, 2 * D])
        zt_f = sb("zt", [P, NB * CH])
        misc = sb("misc", [P, D])
        ident = sb("ident", [P, P])
        qts = sb("qts", [P, CH])
        small = sb("small", [P, 96])
        iota16 = sb("iota16", [P, TOPK])
        sel = sb("sel", [P, 2, TOPK], u32)
        work = sb("work", [P, 1872])
        ps = ctx.enter_context(nc.psum_tensor("ps", [P, 8 * 512], f32))

        A1 = SB * D
        G0 = WS * HALF
        W0 = 0

        def ac(lo, n):
            return act[:, lo:lo + n]

        def bg(lo, n):
            return big[:, lo:lo + n]

        def zn(lo, n):
            return zone[:, lo:lo + n]

        def bank(b, n=512):
            return ps[:, b * 512:b * 512 + n]

        def wk(lo, n):
            return work[:, lo:lo + n]

        def tiles(ap):
            return ap.rearrange("p (k n) -> p k n", k=KT)

        w = bg(W0, WS * HALF).rearrange("p (s k n) -> p s k n", s=WS, k=KT // 2)
        zt = zt_f[:, :].rearrange("p (b n) -> p b n", b=NB)
        acc, hcur = bg(G0 + 4 * D, D), bg(G0 + 5 * D, D)
        a0 = tiles(ac(0, SB * D))
        hT = (tiles(bg(G0, D)), a0[:, :, 0:P], a0[:, :, P:SB * P])
        wide = tiles(ac(0, GROUP[2] * D))
        oT = (tiles(ac(A1, D)), tiles(ac(A1, D)), tiles(ac(A1, GROUP[2] * D)))
        mT = (tiles(ac(A1 + D, D)), tiles(ac(A1 + D, D)), wide)
        h2T = (tiles(ac(A1 + 2 * D, D)), tiles(ac(A1 + 2 * D, D)), wide)
        narrow = ((ac(A1 + 3 * D, D),), hcur, zn(0, D), zn(D, D), acc)
        nbuf = (narrow, narrow,
                ((ac(A1, D), ac(A1 + D, D)), ac(A1 + 2 * D, D), ac(A1 + 3 * D, D), zn(0, D), zn(D, D)),
                ((bg(G0 + D, D), bg(G0 + 2 * D, D)), bg(G0 + 3 * D, D), acc, hcur, zn(0, D)))
        KTB, PTB = A1, A1 + 6400
        QBS, VBS = (G0 + 4 * D + 256, W0 + (SB + 1) * VW), (G0 + D, W0)
        skn = ac(A1 + 3 * D, D)
        onat, tmp4, subg = zn(0, D), zn(D, DH * VD), zn(D + DH * VD, VD)
        QZ, QT = A1, A1 + NB * CH + 2 * CH
        sc2, rep = wk(0, 256), wk(256, 256)
        vals, valsi = wk(512, 32), wk(544, 32).bitcast(u32)
        cand, cand2 = wk(576, 256), wk(832, 256)
        candi, top = wk(1088, 16).bitcast(u32), wk(1104, 16)
        hl = wk(1120, 32).bitcast(u32)
        hlf, vif = wk(1152, 32), wk(1184, 32)
        oh = wk(1216, 512)
        eidx = wk(1728, 32)
        ex16, gel, dots, coef = wk(1760, 16), wk(1776, 16), wk(1792, 16), wk(1808, 16)
        wts = wk(1824, 32)
        ntop, exsum, rsum = wk(1856, 1), wk(1857, 1), wk(1858, 1)

        def slot(g, j):
            return bg((G0 if g < 2 else W0) + (j % RINGS[g // 2]) * D, D)

        w_in_sem = [sem(f"w_loaded{i}") for i in range(WS)]
        w_free = sem("w_free")
        const_ready, ident0, pad_out = sem("const_ready"), sem("ident0"), sem("pad_out")
        dve_s = sem("dve_self")
        mm_done, bank_free = sem("mm_done"), sem("bank_free")
        t_done, t_free = sem("t_done"), sem("t_free")
        cond_in, cond_sig, cond_ready = sem("cond_in"), sem("cond_sig"), sem("cond_ready")
        bada_in, ada_mm, ada_free, ada_out = sem("bada_in"), sem("ada_mm"), sem("ada_free"), [sem(f"ada_out{i}") for i in range(3)]
        nrm = [dict(x=[sem(f"n{s}_x{i}") for i in range(2)], row=sem(f"n{s}_row"), h=sem(f"n{s}_h"))
               for s in range(3)]
        nrm = [dict(nrm[k], base=base, again=again) for k, base, again in ((0, NB, 0), (0, NB + 1, 1), (1, NB + 2, 0), (2, 0, 0))]
        nrm_ms, nrm_rs, h2_out = sem("norm_ms"), sem("norm_rs"), sem("h2_out")
        qk_tab, qn_ms, qn_rs, zo_ready = sem("qk_tab"), sem("qn_ms"), sem("qn_rs"), sem("zo_ready")
        zo_out = [sem(f"zo_out{b}") for b in range(NB)]
        att = [dict(kn=[sem(f"a{s}_kn{i}") for i in range((1, 4)[s])], kt=sem(f"a{s}_kt"), ke=sem(f"a{s}_ke"), v=sem(f"a{s}_v"))
               for s in range(2)]
        for name in ("q", "qt", "qe", "sc", "nm", "ex", "pn", "pt", "pe", "pv", "oe", "ms", "rs", "o", "st"):
            att[0][name] = att[1][name] = sem("att_" + name)
        lam_in, lam_dot, lam_exp = sem("lam_in"), sem("lam_dot"), sem("lam_exp")
        sk_in, sk_t, sk_e = sem("sk_in"), sem("sk_t"), sem("sk_e")
        grp = [dict(nat=[sem(f"g{s}_nat{i}") for i in range(2)], gates=sem(f"g{s}_gates_free"), zt=sem(f"g{s}_zt_used"),
                    br=sem(f"g{s}_br_ready"), br_st=[sem(f"g{s}_br_st{i}") for i in range((1, 3)[s])],
                    g1=sem(f"g{s}_g1"), xt=[sem(f"g{s}_xt{i}") for i in range((1, 3)[s])], ou=sem(f"g{s}_ou_ready"),
                    ou_st=[sem(f"g{s}_ou_st{i}") for i in range(4)], tq=sem(f"g{s}_tq"), te=sem(f"g{s}_te"),
                    sk=sem(f"g{s}_sk"), se=sem(f"g{s}_se"), sc_st=[sem(f"g{s}_sc_st{i}") for i in range(4)])
               for s in range(2)]
        grp = [dict(grp[0], again=0), dict(grp[0], again=1), dict(grp[1], again=0)]
        ring_in = [[sem(f"ring{g}_in{i}") for i in range(RINGS[g])] for g in range(2)]
        ring_free = [sem(f"ring{g}_free") for g in range(2)]
        sc_in, sel_ready, tk_neg, tk_exp, ge_done = sem("sc_in"), sem("sel_ready"), sem("tk_neg"), sem("tk_exp"), sem("ge_done")
        fa_in, fx_in, hn_in, h_taken = sem("fa_in"), sem("fx_in"), sem("hn_in"), sem("h_taken")
        f_ms, f_rs, y_ready, y_out, kv_out = sem("f_ms"), sem("f_rs"), sem("y_ready"), sem("y_out"), sem("kv_out")

        block = ctx.enter_context(nc.Block())

        def block_of(g, lb):
            return (SB, 0, 1 + lb)[g]

        Z0 = (0, QKV_CH)
        NORMED = 3
        ZTS = (2, 2, 3)
        QKV_STEPS = {0: 0, 3: 1, 5: 2, 7: 3}

        def zo(p, c, lb):
            return zn(lb * CH, CH) if p and c >= QKV_CH - 2 else ac(QZ + lb * CH, CH)

        KBUF = 4

        def att_item_tile(b, i):
            return 10 + i * 21 // 16 if b == 0 else 8 + i * 23 // 16

        def gelu_score(b):
            return sum(att_item_tile(b, i) < TOPK for i in range(17)) - 2

        def done_output(sc):
            return sc if sc < 8 else 8 + (sc - 9) // 2 if sc % 2 else None

        @block.sync
        def _(sp):
            final_row = I["final_norm_g"].rearrange("(a n) -> a n", a=1).to_broadcast([P, D])

            def half(n, i, step, ap):
                sp.wait_ge(w_free, n + 1 + i * step)
                sp.nop(nofuse=True)
                sp.dma_start(w[:, n % WS], ap).then_inc(w_in_sem[n % WS], 16)

            def part(t, h, at):
                return t[:, h * (KT // 2):(h + 1) * (KT // 2), ds(at, CH)]

            with sp.Fori(0, ADA_CH // 3) as i:
                for j in range(6):
                    half(j, i, 6, part(w_ada, j % 2, i * (3 * CH) + (j // 2) * CH))
            half(H_QKV[0], 0, 0, part(w_in, 0, 0))
            half(H_QKV[0] + 1, 0, 0, part(w_in, 1, 0))
            for j in range(3):
                sp.wait_ge(ada_out[j], 16 * (ADA_CH // 3))
            s = nrm[3]
            xb, h, A, Bv, gain = nbuf[3]

            def norm1_x(b):
                sp.dma_start(nbuf[3][0][b % 2], xs[b - 1] if b else xp[0]).then_inc(nrm[3]["x"][b % 2], 16)

            sp.dma_start(gain, I["norm1_g"].to_broadcast([P, D])).then_inc(s["row"], 16)
            for c in (1, 0):
                if c == 0:
                    sp.wait_ge(s["h"], 1)
                sp.dma_start(A, mod[c:c + 1, D:2 * D].to_broadcast([P, D])).then_inc(s["row"], 16)
                sp.dma_start(Bv, mod[c:c + 1, 0:D].to_broadcast([P, D])).then_inc(s["row"], 16)
                norm1_x(1 - c)

            def qkv_blocks(p):
                return range(SB) if p else (SB,)

            def qkv(p):
                if p:
                    half(H_QKV[1], 0, 0, part(w_in, 0, 0))
                    half(H_QKV[1] + 1, 0, 0, part(w_in, 1, 0))
                    sp.wait_ge(mm_done, U_QRY[0] + DCH)
                    for i in range(4):
                        sp.wait_ge(grp[0]["sc_st"][i], 16)
                    for b in range(SB):
                        sp.dma_start(ac(QT + b * HD, HD), I["rope_cos"][b * P:(b + 1) * P, :]).then_inc(qk_tab, 16)
                        sp.dma_start(ac(QT + (SB + b) * HD, HD), I["rope_sin"][b * P:(b + 1) * P, :]).then_inc(qk_tab, 16)
                sp.dma_start(ac(QT + 2 * SB * HD, HD), I["q_norm_g"].to_broadcast([P, HD])).then_inc(qk_tab, 16)
                sp.dma_start(ac(QT + 2 * SB * HD + HD, HD), I["k_norm_g"].to_broadcast([P, HD])).then_inc(qk_tab, 16)
                for c in range(QKV_CH):
                    if c + 1 < QKV_CH:
                        for j in range(2):
                            half(H_QKV[p] + 2 * (c + 1) + j, 0, 0, part(w_in, j, (c + 1) * CH))
                    if p and c == QKV_CH - 1:
                        keys(1)
                    for lb, b in enumerate(qkv_blocks(p)):
                        sp.wait_ge(zo_ready, Z0[p] + c * ATT_BLOCKS[p] + lb + SB + 1)
                        sp.dma_start(zs[b, :, c * CH:(c + 1) * CH], zo(p, c, lb)).then_inc(zo_out[b], 16)
                    if p == 0 and c % 2 == 0 and c // 2 + 2 < NB:
                        sp.wait_ge(nrm[3]["h"], c // 2 + 1)
                        norm1_x(c // 2 + 2)

            def keys(p):
                a = att[p]
                if p == 0:
                    sp.wait_ge(nrm[3]["h"], NB)
                else:
                    sp.wait_ge(w_free, H_BR[1] + 3)
                for t in range(SB + 1 if p else 1):
                    if t >= KBUF:
                        sp.wait_ge(a["kt"], 3 * (t - KBUF + 1))
                    at = QBS[p] + (t % KBUF) * NKH * HD
                    blk = t if p else SB
                    cache = t == SB
                    if not cache:
                        sp.wait_ge(zo_out[blk], 16 * (QKV_CH - 2))
                    sp.dma_start(bg(at, KVH * HD), ckg if cache else zs[blk, :, KG0:VG0]).then_inc(a["kn"][t % KBUF], 16)
                    sp.dma_start(bg(at + KVH * HD, 2 * DH * HD), ckd if cache else zs[blk, :, KD0:VD0]).then_inc(a["kn"][t % KBUF], 16)

            def attention(p):
                a = att[p]
                T, blocks = (SB + 1, SB) if p else (1, 1)
                QB, VB = QBS[p], VBS[p]

                def queries(b):
                    blk = b if p else SB
                    sp.dma_start(bg(QB, QH * HD), zs[blk, :, QG0:KG0]).then_inc(a["q"], 16)
                    sp.dma_start(bg(QB + QH * HD, QH * HD), zs[blk, :, QD0:KD0]).then_inc(a["q"], 16)

                if p == 0:
                    sp.wait_ge(zo_out[SB], 16 * QKV_CH)
                    keys(0)
                sp.wait_ge(a["kt"], 3 * T)
                queries(0)
                for b in qkv_blocks(p):
                    sp.wait_ge(zo_out[b], 16 * QKV_CH)
                for t in range(T):
                    blk = t if p else SB
                    cache = t == SB
                    sp.dma_start(bg(VB + t * VW, KVH * HD), cvg if cache else zs[blk, :, VG0:QD0]).then_inc(a["v"], 16)
                    sp.dma_start(bg(VB + t * VW + KVH * HD, DH * VD), cvd if cache else zs[blk, :, VD0:ZW]).then_inc(a["v"], 16)
                sp.dma_start(subg, I["diff_subln_g"].to_broadcast([P, VD])).then_inc(a["v"], 16)
                if p == 0:
                    for dst, lo, n in ((nkg, KG0, KVH * HD), (nvg, VG0, KVH * HD), (nkd, KD0, 2 * DH * HD), (nvd, VD0, DH * VD)):
                        sp.dma_start(dst, zs[SB, :, lo:lo + n]).then_inc(kv_out, 16)
                for b in range(blocks):
                    blk = b if p else SB
                    if b:
                        sp.wait_ge(a["qt"], 4 * (p + b))
                        queries(b)
                        sp.wait_ge(a["o"], p + b)
                        sp.dma_start(osd[blk - 1], onat).then_inc(a["st"], 16)
                sp.wait_ge(a["o"], p + blocks)
                sp.dma_start(osd[blk], onat).then_inc(a["st"], 16)

            for g in range(3):
                n, G, s, R = GROUP[g], grp[g], nrm[g], grp[g]["again"]
                if g < 2:
                    qkv(g)
                    attention(g)

                def br(c, j):
                    at = c * CH
                    return part(w_in, j % 2, at + (ZW if j < 2 else ZW + D)) if j < 4 else part((w_a, w_b)[j - 4], 0, at)

                if g < 2:
                    sp.wait_ge(att[g]["st"], 16 * (1, NB)[g])
                    sp.dma_start(skn.rearrange("p (c d) -> p c d", c=2 * PH), sub).then_inc(sk_in, 16)
                half(H_BR[g], 0, 0, br(0, 0))
                half(H_BR[g] + 1, 0, 0, br(0, 1))
                for lb in range(n):
                    if lb == 0 and g == 2:
                        for i in range(4):
                            sp.wait_ge(grp[1]["sc_st"][i], 32)
                    if lb >= 2:
                        sp.wait_ge(t_done, 4 * (T_O[g] + lb - 1))
                    sp.dma_start(zn((lb % 2) * D, D), osd[block_of(g, lb)]).then_inc(G["nat"][lb % 2], 16)
                if g == 1:
                    sp.dma_start(ac(A1 + 2 * D, D), x1d[SB]).then_inc(fa_in, 16)
                    sp.wait_ge(sk_t, 8)
                    sp.dma_start(ac(A1 + 3 * D, D), mod[1:2, 5 * D:6 * D].to_broadcast([P, D])).then_inc(fa_in, 16)

                def merged_out(c, i):
                    for lb in range(n):
                        sp.wait_ge(G["br"], i * n + (R * DCH + lb + 1))
                        sp.nop(nofuse=True)
                        sp.dma_start(md[block_of(g, lb), :, ds(c * CH, CH)], zn(lb * CH, CH)).then_inc(G["br_st"][lb], 16)

                with sp.Fori(0, DCH - 1) as c:
                    for j in range(2, 6):
                        half(H_BR[g] + j, c, 6, br(c, j))
                    for j in range(2):
                        half(H_BR[g] + 6 + j, c, 6, br(c + 1, j))
                    merged_out(c, c)
                for j in range(2, 6):
                    half(H_BR[g] + 6 * (DCH - 1) + j, 0, 0, br(DCH - 1, j))
                for j in range(2):
                    half(H_OUT[g] + j, 0, 0, part(w_out, j, 0))
                merged_out(DCH - 1, DCH - 1)
                for lb in range(n):
                    sp.wait_ge(G["br_st"][lb], 16 * DCH * (1 + R))
                for lb in range(n):
                    if lb >= 2:
                        sp.wait_ge(t_done, 4 * (T_M[g] + lb - 1))
                    sp.dma_start(zn((lb % 2) * D, D), md[block_of(g, lb)]).then_inc(G["nat"][lb % 2], 16)
                if g == 1:
                    sp.wait_ge(mm_done, U_OUT[1])
                    sp.dma_start(ac(A1, D), final_row).then_inc(fa_in, 16)
                sp.wait_ge(t_done, 4 * (T_M[g] + n))
                cnd = (1, 0, 0)[g]
                sp.dma_start(zn(0, D), mod[cnd:cnd + 1, 2 * D:3 * D].to_broadcast([P, D])).then_inc(G["g1"], 16)
                for c in range(DCH):
                    for lb in range(n):
                        if c:
                            sp.wait_ge(G["ou"], R * DCH + (c - 1) * n + lb + 1)
                        src = (xs[block_of(g, lb)] if g else xp[0])[:, c * CH:(c + 1) * CH]
                        sp.dma_start(zn(D + lb * CH, CH), src).then_inc(G["xt"][lb], 16)
                    for j in range(2):
                        if c < DCH - 1:
                            half(H_OUT[g] + 2 * (c + 1) + j, 0, 0, part(w_out, j, (c + 1) * CH))
                        else:
                            half(H_QRY[g] + j, 0, 0, part(w_qry, j, 0))
                    for lb in range(n):
                        v = c * n + lb
                        sp.wait_ge(G["ou"], R * DCH + v + 1)
                        sp.dma_start(x1d[block_of(g, lb), :, c * CH:(c + 1) * CH], zt[:, v % 4]).then_inc(G["ou_st"][v % 4], 16)
                if g == 1:
                    sp.wait_ge(y_ready, 1)
                    sp.dma_start(yp[0], ac(A1 + 2 * D, D)).then_inc(y_out, 16)
                for i in range(4):
                    sp.wait_ge(G["ou_st"][i], 16 * (n + R))
                xb, h, A, Bv, gain = nbuf[g]
                sp.dma_start(gain, I["norm2_g"].to_broadcast([P, D])).then_inc(s["row"], 16)
                sp.dma_start(A, mod[cnd:cnd + 1, 4 * D:5 * D].to_broadcast([P, D])).then_inc(s["row"], 16)
                sp.dma_start(Bv, mod[cnd:cnd + 1, 3 * D:4 * D].to_broadcast([P, D])).then_inc(s["row"], 16)
                for lb in range(min(2, n)):
                    sp.dma_start(xb[lb], x1d[block_of(g, lb)]).then_inc(s["x"][lb], 16)
                for lb in range(n):
                    if g == 2:
                        sp.wait_ge(s["h"], lb + 1)
                        sp.dma_start(h2d[lb], h).then_inc(h2_out, 16)
                        if lb + 2 < n:
                            sp.dma_start(xb[lb % 2], x1d[block_of(g, lb + 2)]).then_inc(s["x"][lb % 2], 16)
                for c in range(DCH):
                    for j in range(2):
                        if c < DCH - 1:
                            half(H_QRY[g] + 2 * (c + 1) + j, 0, 0, part(w_qry, j, (c + 1) * CH))
                    last = c * n + n if c == DCH - 1 else c * n + n - 2
                    for v in range(max(0, c * n - 2), last):
                        sp.wait_ge(G["se"], R * DCH + v + 1)
                        at = (STEP0[g] + PH * (v % n) + 2 * (v // n)) * VD
                        sp.dma_start(scd[:, at:at + CH], zn((v % 4) * CH, CH)).then_inc(G["sc_st"][v % 4], 16)

            sp.wait_ge(t_done, 4 * (T_H[2] + GROUP[2]))
            sp.wait_ge(h2_out, 16 * GROUP[2])
            sp.dma_start(ac(A1, D), x1d[0]).then_inc(fa_in, 16)
            sp.dma_start(ac(A1 + D, D), mod[0:1, 5 * D:6 * D].to_broadcast([P, D])).then_inc(fa_in, 16)
            sp.dma_start(ac(A1 + 2 * D, D), final_row).then_inc(fa_in, 16)
            sp.wait_ge(mm_done, U_QRY[2] + DCH * GROUP[2])
            sp.dma_start(ac(2 * D, D), h2d[0]).then_inc(hn_in, 16)
            sp.dma_start(ac(0, D), x1d[1]).then_inc(fx_in, 16)
            sp.dma_start(ac(D, D), mod[0:1, 5 * D:6 * D].to_broadcast([P, D])).then_inc(fx_in, 16)
            sp.wait_ge(y_ready, 2)
            sp.dma_start(ys[0], ac(A1, D)).then_inc(y_out, 16)
            for b in range(GROUP[2]):
                if b + 1 < GROUP[2]:
                    sp.wait_ge(h_taken, b + 1)
                    sp.dma_start(ac(2 * D, D), h2d[b + 1]).then_inc(hn_in, 16)
                sp.wait_ge(y_ready, b + 3)
                sp.dma_start(ys[b + 1], ac(0, D)).then_inc(y_out, 16)
                sp.wait_ge(y_out, 16 * (b + 3))
                if b + 1 < GROUP[2]:
                    sp.dma_start(ac(0, D), x1d[b + 2]).then_inc(fx_in, 16)

        @block.gpsimd
        def _(pool):
            pool.dma_start(small[:, 0:16], I["c"].rearrange("a (p t) -> (a p) t", p=P)).then_inc(cond_in, 16)
            pool.dma_start(small[:, 16:32], I["c_ctx"].rearrange("(p t) -> p t", p=P)).then_inc(cond_in, 16)
            pool.dma_start(act[0:2, 0:6 * D], I["b_ada"].to_broadcast([2, 6 * D])).then_inc(bada_in, 16)
            for n, v in enumerate(("lambda_q1", "lambda_k1", "lambda_q2", "lambda_k2")):
                pool.dma_start(misc[:, n * HD:(n + 1) * HD], I[v].to_broadcast([P, HD])).then_inc(lam_in, 16)
            nc.gpsimd.memset(ident[:, :], 0.0).then_inc(ident0, 1)
            pool.wait_ge(ident0, 1)
            nc.gpsimd.affine_select(out=ident[:, :], in_=ident[:, :], compare_op=ALU.not_equal, fill=1.0, base=0,
                                    pattern=[[-1, P]], channel_multiplier=1).then_inc(const_ready, 1)
            nc.gpsimd.iota(iota16[:, :], pattern=[[1, TOPK]], base=0, channel_multiplier=0,
                           allow_small_or_imprecise_dtypes=True).then_inc(const_ready, 1)
            pool.wait_ge(const_ready, 2)
            for i in range(2):
                pool.dma_start(scd[:, STEPS * VD + i * P:STEPS * VD + (i + 1) * P], ident[:, :]).then_inc(pad_out, 16)

            with pool.Fori(0, ADA_CH // 3) as i:
                for j in range(3):
                    pool.wait_ge(ada_free, i * 3 + j + 4)
                    pool.nop(nofuse=True)
                    pool.dma_start(mod[:, ds(i * (3 * CH) + j * CH, CH)], zt[0:2, j]).then_inc(ada_out[j], 16)
            def scores_in(step):
                pool.dma_start(sc2, scd[:, ds(step * VD, VD)]).then_inc(sc_in, 16)

            def gathers(g, step, q, at, ahead=True):
                pool.wait_ge(sel_ready, step + 1)
                pool.nop(nofuse=True)
                if ahead:
                    scores_in(step + 1)
                for j in range(2 * TOPK):
                    pool.wait_ge(ring_free[g // 2], at + j + 1)
                    pool.nop(nofuse=True)
                    pool.indirect_dma_start(
                        slot(g, j), None, eu if j < TOPK else ev,
                        bass.IndirectOffsetOnAxis(ap=sel[:, q, j % TOPK:j % TOPK + 1], axis=0)).then_inc(ring_in[g // 2][j % RINGS[g // 2]], 16)

            for g in range(3):
                for i in range(4):
                    pool.wait_ge(grp[g]["sc_st"][i], 16 * (GROUP[g] + grp[g]["again"]))
                if g:
                    pool.wait_ge(sel_ready, STEP0[g])
                if g == 2:
                    pool.wait_ge(pad_out, 32)
                scores_in(STEP0[g])
                steps, before = PH * GROUP[g], (0, PH, 0)[g]
                with pool.Fori(0, steps // 2 - (g < 2)) as i:
                    for q in range(2):
                        gathers(g, i * 2 + STEP0[g] + q, q, i * (4 * TOPK) + (before + q) * 2 * TOPK)
                if g < 2:
                    for q in range(2):
                        gathers(g, STEP0[g] + PH - 2 + q, q, (before + PH - 2 + q) * 2 * TOPK, ahead=q == 0)
            pool.wait_ge(kv_out, 16 * 4)

        @block.tensor
        def _(pe):
            def wait_half(n, i, step):
                pe.wait_ge(w_in_sem[n % WS], 16 * (n // WS + 1) + i * (16 * step // WS))

            def products(acts, b, n, bk, start, stop):
                for k in range(KT // 2):
                    ins = nc.tensor.matmul(bank(bk), acts[:, k, b * P:(b + 1) * P], w[:, n % WS, k],
                                           start=(start and k == 0), stop=(stop and k == KT // 2 - 1))
                return ins

            def chunk(acts, n, i, step, blocks, u, bank_of, depth):
                for h in range(2):
                    wait_half(n + h, i, step)
                    for b in range(blocks):
                        if h == 0:
                            pe.wait_ge(bank_free, u + b + 1 + NB - depth)
                        ins = products(acts[:, h * (KT // 2):(h + 1) * (KT // 2)], b, n + h, bank_of(b), h == 0, h == 1)
                        if h == 1:
                            ins.then_inc(mm_done, 1)
                    if h == 0:
                        ins.then_inc(w_free, 1)
                release(u + blocks)

            def release(u):
                pe.wait_ge(mm_done, u)
                pe.sem_inc(w_free, 1)

            def transposes(B, src):
                for q in range(4):
                    pe.wait_ge(t_free, B * 4 + q + 1)
                    for k in range(4):
                        ins = nc.tensor.transpose(ps[:, (4 + q) * 512 + k * P:(4 + q) * 512 + (k + 1) * P],
                                                  src[:, (4 * q + k) * P:(4 * q + k + 1) * P], ident[:, :])
                    ins.then_inc(t_done, 1)

            pe.sem_inc(w_free, WS)
            pe.sem_inc(att[0]["pv"], 2)
            pe.wait_ge(cond_ready, 1)
            cond = small[:, 64:96].rearrange("p (t c) -> p t c", c=2)
            with pe.Fori(0, ADA_CH // 3) as i:
                for j in range(3):
                    pe.wait_ge(ada_free, i * 3 + j + 1)
                    pe.nop(nofuse=True)
                    for h in range(2):
                        wait_half(2 * j + h, i, 6)
                        for k in range(KT // 2):
                            ins = nc.tensor.matmul(ps[0:2, j * 512:(j + 1) * 512], cond[:, h * (KT // 2) + k], w[:, (2 * j + h) % WS, k],
                                                   start=(h + k == 0), stop=(h == 1 and k == KT // 2 - 1))
                        ins.then_inc(ada_mm if h else w_free, 1)
                    pe.wait_ge(ada_mm, i * 3 + j + 1)
                    pe.sem_inc(w_free, 1)
            def norm1_turn(b):
                pe.wait_ge(nrm[3]["h"], b + 1)
                transposes(b, nbuf[3][1])

            pe.wait_ge(const_ready, 2)
            norm1_turn(0)
            pe.wait_ge(t_free, 4 + 4)
            pe.wait_ge(ada_free, 3 + ADA_CH)

            def qkv(p):
                if p:
                    pe.wait_ge(t_free, NB * 4 + 4)
                    with pe.Fori(0, QKV_CH // 3) as i:
                        for j in range(3):
                            chunk(a0, H_QKV[1] + 2 * j, i, 6, SB, i * (3 * SB) + (U_QKV[1] + j * SB), lambda b: b, 4)
                else:
                    for c in range(QKV_CH):
                        chunk(hT[0], H_QKV[0] + 2 * c, 0, 0, 1, U_QKV[0] + c, lambda b: c % 4, 4)
                        if c % 2:
                            norm1_turn(c // 2 + 1)

            def attention(p):
                a = att[p]
                T, blocks = (SB + 1, SB) if p else (1, 1)
                QB, VB = QBS[p], VBS[p]
                kT = ac(KTB, NKH * T * P).rearrange("p (h n) -> p h n", h=NKH)
                qT = misc[:, :].rearrange("p (h n) -> p h n", h=16)
                for t in range(T):
                    pe.wait_ge(a["kn"][t % KBUF], 32 * (t // KBUF + 1))
                    if t:
                        pe.wait_ge(a["ke"], 3 * t)
                    for g, n in enumerate((4, 4, 2)):
                        for j in range(n):
                            at = QB + (t % KBUF) * NKH * HD + (4 * g + j) * HD
                            ins = nc.tensor.transpose(bank(4 + g, 512)[:, j * P:(j + 1) * P], bg(at, HD), ident[:, :])
                        ins.then_inc(a["kt"], 1)
                pe.wait_ge(a["ke"], 3 * T)
                pe.wait_ge(bank_free, U_QKV[p] + QKV_CH * blocks + NB)

                with pe.Fori(0, blocks) as i:
                    qb = i + p
                    def scores(sc):
                        kh = sc // 4 if sc < 8 else KVH + sc - 8
                        pe.wait_ge(a["ex"], qb * 16 + sc + 1)
                        lo = (sc % 2) * 1024
                        for c0 in range(0, T * P, 512):
                            n = min(512, T * P - c0)
                            ins = nc.tensor.matmul(ps[:, lo + c0:lo + c0 + n], qT[:, sc], kT[:, kh, c0:c0 + n], start=True, stop=True)
                        ins.then_inc(a["sc"], 1)

                    def turn_weights(o, sc):
                        pe.wait_ge(a["pn"], qb * 12 + o + 1)
                        if o:
                            pe.wait_ge(a["pe"], qb * 12 + o)
                        for t in range(T):
                            ins = nc.tensor.transpose(ps[:, 2048 + t * P:2048 + (t + 1) * P],
                                                      zt_f[:, (sc % 4) * 640 + t * P:(sc % 4) * 640 + (t + 1) * P], ident[:, :])
                        ins.then_inc(a["pt"], 1)

                    def output(o):
                        pe.wait_ge(a["pe"], qb * 12 + o + 1)
                        if o == 0:
                            pe.wait_ge(a["v"], 32 * T + 16)
                        if o >= 2:
                            pe.wait_ge(a["oe"], qb * 12 + o + 1)
                        v0, vn = ((o // 4) * HD, HD) if o < 8 else (KVH * HD + (o - 8) * VD, VD)
                        for t in range(T):
                            ins = nc.tensor.matmul(bank(6 + o % 2, vn), ac(PTB + (o % 2) * 640 + t * P, P), bg(VB + t * VW + v0, vn),
                                                   start=(t == 0), stop=(t == T - 1))
                        ins.then_inc(a["pv"], 1)

                    pe.wait_ge(a["q"], qb * 32 + 32)
                    pe.wait_ge(a["oe"], qb * 12 + 2)
                    for g in range(4):
                        for j in range(4):
                            ins = nc.tensor.transpose(bank(4 + g, 512)[:, j * P:(j + 1) * P], bg(QB + (4 * g + j) * HD, HD), ident[:, :])
                        ins.then_inc(a["qt"], 1)
                    pe.wait_ge(a["qe"], qb * 4 + 4)
                    scores(0)
                    scores(1)
                    for sc in range(16):
                        if sc + 2 < 16:
                            scores(sc + 2)
                        o = done_output(sc)
                        if o is not None:
                            turn_weights(o, sc)
                            if o:
                                output(o - 1)
                    output(11)

            for g in range(3):
                n, G, R = GROUP[g], grp[g], grp[g]["again"]
                if g < 2:
                    qkv(g)
                    attention(g)
                    pe.wait_ge(att[g]["oe"], 12 * (1, NB)[g] + 2)
                    pe.wait_ge(sk_in, 16 * (g + 1))
                    for i in range(4):
                        for j in range(4):
                            ins = nc.tensor.transpose(bank(4 + i)[:, j * P:(j + 1) * P], skn[:, (4 * i + j) * HD:(4 * i + j + 1) * HD], ident[:, :])
                        ins.then_inc(sk_t, 1)
                    pe.wait_ge(sk_e, 4 * (g + 1))

                def bk(v):
                    return v % 4

                for lb in range(n):
                    pe.wait_ge(G["nat"][lb % 2], 16 * (2 * R + lb // 2 + 1))
                    transposes(T_O[g] + lb, zn((lb % 2) * D, D))
                pe.wait_ge(t_free, (T_O[g] + n) * 4 + 4)
                with pe.Fori(0, DCH) as c:
                    u = c * (4 * n) + U_BR[g]
                    for p_ in range(2):
                        chunk(hT[g], H_BR[g] + 2 * p_, c, 6, n, u + p_ * n, lambda b: bk(p_ * n + b), 4)
                    for p_ in range(2):
                        nh = H_BR[g] + 4 + p_
                        wait_half(nh, c, 6)
                        for b in range(n):
                            v = (2 + p_) * n + b
                            pe.wait_ge(bank_free, u + (v + 2))
                            products(oT[g][:, p_ * (KT // 2):(p_ + 1) * (KT // 2)], b, nh, bk(v), True, True).then_inc(mm_done, 1)
                        release(u + (3 + p_) * n)
                for lb in range(n):
                    first = (n + 1 - lb % 2) // 2
                    pe.wait_ge(G["nat"][lb % 2], 16 * (2 * R + first + lb // 2 + 1))
                    transposes(T_M[g] + lb, zn((lb % 2) * D, D))
                pe.wait_ge(t_free, (T_M[g] + n) * 4 + 4)
                for c in range(DCH):
                    chunk(mT[g], H_OUT[g] + 2 * c, 0, 0, n, U_OUT[g] + c * n, lambda b: bk(c * n + b), 4)
                for lb in range(n):
                    pe.wait_ge(nrm[g]["h"], R + lb + 1)
                    transposes(T_H[g] + lb, nbuf[g][1])
                pe.wait_ge(t_free, (T_H[g] + n) * 4 + 4)

                units = DCH * n

                def turn(v):
                    pe.wait_ge(bank_free, U_QRY[g] + v + NB + 1)
                    if v:
                        pe.wait_ge(G["te"], R * DCH + v)
                    for q in range(4):
                        ins = nc.tensor.transpose(bank(5)[:, q * P:(q + 1) * P], zt[:, v % 4, q * P:(q + 1) * P], ident[:, :])
                    ins.then_inc(G["tq"], 1)

                def keys(v):
                    pe.wait_ge(G["te"], R * DCH + v + 1)
                    if v:
                        pe.wait_ge(G["se"], R * DCH + v)
                    for q in range(4):
                        at = (4 * (v // n) + q) * P
                        ins = nc.tensor.matmul(bank(6)[:, q * P:(q + 1) * P], qts[:, q * P:(q + 1) * P], misc[:, at:at + P], start=True, stop=True)
                    ins.then_inc(G["sk"], 1)

                for c in range(DCH):
                    nh = H_QRY[g] + 2 * c
                    for h in range(2):
                        wait_half(nh + h, 0, 0)
                        for b in range(n):
                            v = c * n + b
                            if h == 0:
                                pe.wait_ge(bank_free, U_QRY[g] + v + 2)
                            ins = products(h2T[g][:, h * (KT // 2):(h + 1) * (KT // 2)], b, nh + h, bk(v), h == 0, h == 1)
                            if h == 1:
                                ins.then_inc(mm_done, 1)
                                if v >= 1:
                                    turn(v - 1)
                                if v >= 2:
                                    keys(v - 2)
                        if h == 0:
                            ins.then_inc(w_free, 1)
                    release(U_QRY[g] + (c + 1) * n)
                turn(units - 1)
                keys(units - 2)
                keys(units - 1)

        @block.scalar
        def _(sa):
            def evac(u, bk, to, func=ACT.Copy):
                sa.wait_ge(mm_done, u + 1)
                nc.scalar.activation(to, bank(bk), func).then_inc(bank_free, 1)

            def transposed(B, b, dst):
                for q in range(4):
                    sa.wait_ge(t_done, B * 4 + q + 1)
                    nc.scalar.activation(dst[:, 4 * q:4 * q + 4, b * P:(b + 1) * P],
                                         bank(4 + q).rearrange("p (k n) -> p k n", k=4), ACT.Copy).then_inc(t_free, 1)

            def root(s, b):
                sa.wait_ge(nrm_ms, s["base"] + b + 1)
                nc.scalar.activation(small[:, 1:2], small[:, 0:1], ACT.Sqrt).then_inc(nrm_rs, 1)

            def top_exps(step):
                sa.wait_ge(tk_neg, step + 1)
                nc.scalar.activation(ex16, top, ACT.Exp, bias=ntop, accum_out=exsum).then_inc(tk_exp, 1)

            def gelus(g, at):
                sa.wait_ge(ring_free[g // 2], at + RINGS[g // 2] + TOPK)
                nc.scalar.activation(gel, dots, ACT.Gelu).then_inc(ge_done, 1)

            def final_root(nth):
                sa.wait_ge(f_ms, nth)
                nc.scalar.activation(small[:, 1:2], small[:, 0:1], ACT.Sqrt).then_inc(f_rs, 1)

            sa.sem_inc(bank_free, NB)
            sa.sem_inc(t_free, 4)
            sa.sem_inc(att[0]["ex"], 2)
            sa.wait_ge(cond_in, 32)
            nc.scalar.activation(small[:, 32:64], small[:, 0:32], ACT.Sigmoid).then_inc(cond_sig, 1)
            sa.wait_ge(lam_dot, 1)
            nc.scalar.activation(small[:, 4:6], small[:, 4:6], ACT.Exp).then_inc(lam_exp, 1)
            root(nrm[3], 0)
            transposed(0, 0, hT[0])

            def qkv(p):
                n = ATT_BLOCKS[p]
                for c in range(QKV_CH):
                    for lb in range(n):
                        x = c * n + lb
                        sa.wait_ge(zo_ready, Z0[p] + x + (1 if p else SB))
                        evac(U_QKV[p] + x, x % 4, zt[:, lb])
                        if c < NORMED:
                            sa.wait_ge(qn_ms, NORMED * p + x + 1)
                            nc.scalar.activation(small[:, 12:16], small[:, 8:12], ACT.Sqrt).then_inc(qn_rs, 1)
                    if p == 0 and c < 2 * SB:
                        if c % 2 == 0:
                            root(nrm[3], c // 2 + 1)
                        else:
                            transposed(c // 2 + 1, c // 2, a0)
                    if p and c in QKV_STEPS:
                        top_exps(QKV_STEPS[c] + 1)
                        gelus(0, QKV_STEPS[c] * 2 * TOPK)

            def attention(p):
                a = att[p]
                T, blocks = (SB + 1, SB) if p else (1, 1)
                kT = ac(KTB, NKH * T * P).rearrange("p (h n) -> p h n", h=NKH)
                for t in range(T):
                    for g, n in enumerate((4, 4, 2)):
                        sa.wait_ge(a["kt"], 3 * t + g + 1)
                        nc.scalar.activation(kT[:, 4 * g:4 * g + n, t * P:(t + 1) * P],
                                             bank(4 + g, n * P).rearrange("p (h n) -> p h n", h=n), ACT.Copy).then_inc(a["ke"], 1)
                sa.wait_ge(zo_ready, Z0[p] + QKV_CH * blocks + SB)

                def diff_root(qb):
                    sa.wait_ge(a["ms"], qb + 1)
                    nc.scalar.activation(small[:, 12:16], small[:, 8:12], ACT.Sqrt).then_inc(a["rs"], 1)

                for i in range(blocks):
                    qb = i + p
                    def exps(sc):
                        if sc < 4:
                            last = 8 + (sc + 4) // 2
                            sa.wait_ge(a["pt"], qb * 12 + last + 1)
                        else:
                            last = sc - 4 if sc - 4 < 8 else 8 + (sc - 12) // 2
                            sa.wait_ge(a["pt"], qb * 12 + 12 + last + 1)
                        sa.wait_ge(a["nm"], qb * 16 + sc + 1)
                        lo, sl = (sc % 2) * 1024, sc % 4
                        nc.scalar.activation(zt_f[:, sl * 640:sl * 640 + T * P], ps[:, lo:lo + T * P], ACT.Exp,
                                             bias=small[:, 16 + sl:17 + sl], scale=SCALE,
                                             accum_out=small[:, 20 + sl:21 + sl]).then_inc(a["ex"], 1)

                    for g in range(4):
                        sa.wait_ge(a["qt"], qb * 4 + g + 1)
                        nc.scalar.activation(misc[:, g * 512:(g + 1) * 512], bank(4 + g), ACT.Copy).then_inc(a["qe"], 1)
                    if i:
                        diff_root(qb - 1)
                    exps(0)
                    exps(1)
                    for sc in range(16):
                        o = done_output(sc)
                        if o is not None:
                            sa.wait_ge(a["pt"], qb * 12 + 12 + o + 1)
                            sa.wait_ge(a["pv"], qb * 12 + o + 1)
                            nc.scalar.activation(ac(PTB + (o % 2) * 640, T * P), ps[:, 2048:2048 + T * P], ACT.Copy).then_inc(a["pe"], 1)
                        if sc + 2 < 16:
                            exps(sc + 2)
                        if p and sc == gelu_score(i):
                            if i + 1 < blocks:
                                top_exps(i + 5)
                                gelus(0, (i + 4) * 2 * TOPK)
                diff_root(p + blocks - 1)

            for g in range(3):
                n, G, R = GROUP[g], grp[g], grp[g]["again"]
                if g < 2:
                    qkv(g)
                    attention(g)
                    for i in range(4):
                        sa.wait_ge(sk_t, 4 * g + i + 1)
                        nc.scalar.activation(misc[:, i * 512:(i + 1) * 512], bank(4 + i), ACT.Copy).then_inc(sk_e, 1)
                for lb in range(n):
                    transposed(T_O[g] + lb, lb, oT[g])
                def branch(c):
                    u = c * (4 * n) + U_BR[g]
                    for p_ in range(2):
                        for lb in range(n):
                            if p_ == 0:
                                sa.wait_ge(G["gates"], c * n + (R * DCH + lb + 1))
                            v = p_ * n + lb
                            evac(u + v, v % 4, zn((p_ * SB + lb) * CH, CH), ACT.Sigmoid)
                        if g == 2 and p_ == 0:
                            top_exps(c + (PH + 1))
                            gelus(1, c * (2 * TOPK) + PH * 2 * TOPK)
                    for p_ in range(2):
                        for lb in range(n):
                            v = (2 + p_) * n + lb
                            sa.wait_ge(G["zt"], c * (2 * n) + (2 * DCH * R + p_ * n + lb + 1))
                            evac(u + v, v % 4, zt[:, (p_ * n + lb) % ZTS[g]])

                if g == 1:
                    for c in range(DCH):
                        branch(c)
                        if c == 1:
                            gelus(0, 7 * 2 * TOPK)
                else:
                    with sa.Fori(0, DCH) as c:
                        branch(c)
                for lb in range(n):
                    transposed(T_M[g] + lb, lb, mT[g])
                if g == 1:
                    final_root(1)
                for c in range(DCH):
                    for lb in range(n):
                        v = c * n + lb
                        if v == 0:
                            sa.wait_ge(G["zt"], 2 * DCH * (n + R) + ZTS[g])
                        if v >= 4:
                            sa.wait_ge(G["ou_st"][v % 4], 16 * (v // 4))
                        evac(U_OUT[g] + v, v % 4, zt[:, v % 4])
                        if g == 2 and v in (2, 8):
                            step = PH + 4 + v // 6
                            top_exps(step + 1)
                            gelus(1, step * 2 * TOPK)
                for lb in range(n):
                    root(nrm[g], lb)
                    if g == 1:
                        sa.wait_ge(y_out, 16)
                    transposed(T_H[g] + lb, lb, h2T[g])
                if g == 2:
                    top_exps(PH + 7)
                    gelus(1, (PH + 6) * 2 * TOPK)
                units = DCH * n
                for v in range(units + 2):
                    if v < units:
                        if v >= 4:
                            sa.wait_ge(G["tq"], v - 3)
                        evac(U_QRY[g] + v, v % 4, zt[:, v % 4])
                    if 1 <= v <= units:
                        sa.wait_ge(G["tq"], R * DCH + v)
                        if v >= 2:
                            sa.wait_ge(G["sk"], R * DCH + v - 1)
                        nc.scalar.activation(qts[:, :], bank(5), ACT.Copy).then_inc(G["te"], 1)
                    if v >= 2:
                        x = v - 2
                        sa.wait_ge(G["sk"], R * DCH + x + 1)
                        if x >= 4:
                            sa.wait_ge(G["sc_st"][x % 4], 16 * (x // 4))
                        nc.scalar.activation(zn((x % 4) * CH, CH), bank(6), ACT.Copy).then_inc(G["se"], 1)
                    if g == 2 and v == 9:
                        gelus(1, (PH + 7) * 2 * TOPK)
                if g < 2:
                    top_exps(STEP0[g])
            top_exps(2 * PH)
            final_root(2)
            with sa.Fori(0, GROUP[2]) as b:
                with sa.Fori(0, PH) as h:
                    m = b * PH + h
                    top_exps(m + 2 * PH + 1)
                    gelus(2, m * (2 * TOPK))
                final_root(b + 3)

        @block.vector
        def _(dve):
            ch = Chain(dve, dve_s)
            link = ch.link
            V = nc.vector

            def signal(ins, s, value):
                ins.then_inc(s, 1)
                dve.wait_ge(s, value)

            for s_, n in ((ada_free, 3), (zo_ready, SB), (grp[0]["gates"], 1), (grp[2]["gates"], GROUP[2]), (grp[0]["zt"], ZTS[0]),
                          (grp[2]["zt"], ZTS[2]), (att[0]["pt"], 12), (att[0]["oe"], 2)):
                dve.sem_inc(s_, n)
            dve.wait_ge(cond_sig, 1)
            signal(V.tensor_tensor(small[:, 64:96].rearrange("p (t c) -> p c t", c=2), small[:, 0:32].rearrange("p (c t) -> p c t", c=2),
                                   small[:, 32:64].rearrange("p (c t) -> p c t", c=2), ALU.mult), cond_ready, 1)
            dve.wait_ge(lam_in, 64)
            for n in range(2):
                link(V.tensor_tensor_reduce(out=misc[:, 512:512 + HD], in0=misc[:, 2 * n * HD:(2 * n + 1) * HD],
                                            in1=misc[:, (2 * n + 1) * HD:(2 * n + 2) * HD], scale=1.0, scalar=0.0,
                                            op0=ALU.mult, op1=ALU.add, accum_out=small[:, 4 + n:5 + n]))
            dve.sem_inc(lam_dot, 1)
            dve.wait_ge(lam_exp, 1)
            link(V.tensor_tensor(small[:, 6:7], small[:, 5:6], small[:, 4:5], ALU.subtract))
            link(V.tensor_scalar(small[:, 6:7], small[:, 6:7], -LAM_INIT, None, ALU.add))
            dve.wait_ge(bada_in, 16)
            with dve.Fori(0, ADA_CH // 3) as i:
                for j in range(3):
                    dve.wait_ge(ada_mm, i * 3 + j + 1)
                    dve.nop(nofuse=True)
                    V.tensor_tensor(zt[0:2, j], ps[0:2, j * 512:(j + 1) * 512], act[0:2, ds(i * (3 * CH) + j * CH, CH)],
                                    ALU.add).then_inc(ada_free, 1)
                for j in range(3):
                    dve.wait_ge(ada_out[j], i * 16 + 16)
            dve.wait_ge(ada_free, 3 + ADA_CH)

            def norm(s, g, b, T0):
                xb, h, A, Bv, gain = nbuf[g]
                R, x = s["again"], xb[b % 2]
                if b == 0 or (b == 1 and g == 3):
                    dve.wait_ge(s["row"], 48 * (1 + R) if b == 0 else 80)
                    link(V.scalar_tensor_tensor(A, A, 1.0, gain, ALU.add, ALU.mult))
                dve.wait_ge(s["x"][b % 2], 16 * (b // 2 + 1 + R))
                if b:
                    dve.wait_ge(t_done, 4 * (T0 + b))
                    if g == 2:
                        dve.wait_ge(h2_out, 16 * b)
                link(V.tensor_tensor_reduce(out=h, in0=x, in1=x, scale=1.0, scalar=0.0, op0=ALU.mult, op1=ALU.add,
                                            accum_out=small[:, 2:3]))
                signal(V.tensor_scalar(small[:, 0:1], small[:, 2:3], 1.0 / D, EPS, ALU.mult, ALU.add), nrm_ms, s["base"] + b + 1)
                dve.wait_ge(nrm_rs, s["base"] + b + 1)
                link(V.reciprocal(small[:, 3:4], small[:, 1:2]))
                link(V.scalar_tensor_tensor(h, x, small[:, 3:4], A, ALU.mult, ALU.mult))
                signal(V.tensor_tensor(h, h, Bv, ALU.add), s["h"], R + b + 1)

            norm(nrm[3], 3, 0, 0)

            t1, t2 = ac(QZ + NB * CH, CH), ac(QZ + (NB + 1) * CH, CH)
            qgain, kgain = ac(QT + 2 * SB * HD, HD), ac(QT + 2 * SB * HD + HD, HD)

            def hview(ap, h):
                return ap.rearrange("p (h d) -> p h d", h=h)

            def halves(ap, h):
                return ap.rearrange("p (h a e d) -> p h a e d", h=h, a=2, e=2)

            def head_norm(u, b, nh, g):
                z = zt[:, b, 0:nh * HD]
                link(V.tensor_tensor(t1[:, 0:nh * HD], z, z, ALU.mult))
                link(V.tensor_reduce(small[:, 28:28 + nh], hview(t1[:, 0:nh * HD], nh), AX.X, ALU.add))
                signal(V.tensor_scalar(small[:, 8:8 + 4], small[:, 28:32], 1.0 / HD, EPS, ALU.mult, ALU.add), qn_ms, u + 1)
                dve.wait_ge(qn_rs, u + 1)
                link(V.reciprocal(small[:, 24:28], small[:, 12:16]))
                link(V.tensor_tensor(hview(z, nh), hview(z, nh), small[:, 24:24 + nh].unsqueeze(2).to_broadcast([P, nh, HD]), ALU.mult))
                link(V.tensor_tensor(hview(z, nh), hview(z, nh), g.unsqueeze(1).to_broadcast([P, nh, HD]), ALU.mult))

            def finish(x, b, rot, to):
                if rot:
                    cos = ac(QT + b * HD, HD)
                    sin = ac(QT + SB * HD + b * HD, HD).rearrange("p (a e d) -> p a e d", a=2, e=2)
                    z, n = zt[:, b, 0:rot * HD], rot * HD
                    link(V.tensor_tensor(hview(t1[:, 0:n], rot), hview(z, rot), cos.unsqueeze(1).to_broadcast([P, rot, HD]), ALU.mult))
                    for e in range(2):
                        link(V.tensor_tensor(halves(t2[:, 0:n], rot)[:, :, :, e], halves(z, rot)[:, :, :, 1 - e],
                                             sin[:, :, e].unsqueeze(1).to_broadcast([P, rot, 2, HD // 4]), ALU.mult))
                    if rot < 4:
                        link(V.tensor_copy(to[:, n:CH], zt[:, b, n:CH]))
                    ins = V.tensor_tensor(to[:, 0:n], t1[:, 0:n], t2[:, 0:n], ALU.add)
                else:
                    ins = V.tensor_copy(to, zt[:, b])
                signal(ins, zo_ready, x + SB + 1)

            def stored(sems, count):
                for s_ in sems:
                    dve.wait_ge(s_, count)

            def pick(src, spare, v16, i16):
                for half in range(2):
                    s_ = src if half == 0 else spare
                    v8, i8 = v16[:, 8 * half:8 * half + 8], i16[:, 8 * half:8 * half + 8]
                    dve.nop(nofuse=True)
                    link(V.max(out=v8, in_=s_))
                    dve.nop(nofuse=True)
                    link(V.max_index(out=i8, in_max=v8, in_values=s_))
                    if half == 0:
                        dve.nop(nofuse=True)
                        link(V.match_replace(out=spare, in_to_replace=v8, in_values=src, imm_value=NEG))

            def choose(step, q):
                dve.wait_ge(sc_in, step * 16 + 16)
                for c in range(2):
                    pick(sc2[:, c * NK:(c + 1) * NK], rep[:, c * NK:(c + 1) * NK], vals[:, c * 16:c * 16 + 16], valsi[:, c * 16:c * 16 + 16])
                link(V.tensor_tensor(cand.rearrange("p (i j) -> p i j", i=TOPK), vals[:, 0:16].unsqueeze(2).to_broadcast([P, TOPK, TOPK]),
                                     vals[:, 16:32].unsqueeze(1).to_broadcast([P, TOPK, TOPK]), ALU.add))
                pick(cand, cand2, top, candi)
                V.tensor_scalar(ntop, top[:, 0:1], -1.0, None, ALU.mult).then_inc(tk_neg, 1)
                link(V.tensor_scalar(hl[:, 0:16], candi, 4, None, ALU.logical_shift_right))
                link(V.tensor_scalar(hl[:, 16:32], candi, 15, None, ALU.bitwise_and))
                link(V.tensor_copy(hlf, hl))
                link(V.tensor_copy(vif, valsi))
                o4 = oh.rearrange("p (c w j) -> p c w j", c=2, w=TOPK)
                for c in range(2):
                    link(V.tensor_tensor(o4[:, c], hlf[:, c * 16:c * 16 + 16].unsqueeze(2).to_broadcast([P, TOPK, TOPK]),
                                         iota16[:, :].unsqueeze(1).to_broadcast([P, TOPK, TOPK]), ALU.is_equal))
                    link(V.tensor_tensor(o4[:, c], o4[:, c], vif[:, c * 16:c * 16 + 16].unsqueeze(1).to_broadcast([P, TOPK, TOPK]), ALU.mult))
                link(V.tensor_reduce(eidx, oh.rearrange("p (w j) -> p w j", j=TOPK), AX.X, ALU.add))
                link(V.scalar_tensor_tensor(sel[:, q], eidx[:, 0:16], float(NK), eidx[:, 16:32], ALU.mult, ALU.add))
                dve.wait_ge(tk_exp, step + 1)
                link(V.reciprocal(rsum, exsum))
                signal(V.tensor_scalar(wts[:, q * 16:q * 16 + 16], ex16, rsum, None, ALU.mult), sel_ready, step + 1)

            CHOOSE = 5 * 3 + 1 + 4 + 4 + 2 + 1
            STEP = CHOOSE + 1

            def peer_step(g, step, q, m, ahead=True, during=None):
                ring, R = g // 2, RINGS[g // 2]
                for k in range(TOPK):
                    dve.wait_ge(ring_in[ring][k % R], m * (32 // R * 16) + (k // R + 1) * 16)
                    t = slot(g, k)
                    V.tensor_tensor_reduce(out=t, in0=t, in1=hcur, scale=1.0, scalar=0.0, op0=ALU.mult, op1=ALU.add,
                                           accum_out=dots[:, k:k + 1]).then_inc(ring_free[ring], 1)
                    if during:
                        during(k)
                if ahead:
                    choose(step + 1, 1 - q)
                dve.wait_ge(ge_done, step + 1)
                link(V.tensor_tensor(coef, gel, wts[:, q * 16:q * 16 + 16], ALU.mult))
                for k in range(TOPK):
                    dve.wait_ge(ring_in[ring][k % R], m * (32 // R * 16) + ((TOPK + k) // R + 1) * 16)
                    signal(V.scalar_tensor_tensor(acc, slot(g, k), coef[:, k:k + 1], acc, ALU.mult, ALU.add),
                           ring_free[ring], m * 32 + R + TOPK + k + 1)
                    if during:
                        during(TOPK + k)

            def final(x1, gate, gain, nth):
                link(V.tensor_tensor(acc, acc, gate, ALU.mult))
                link(V.tensor_tensor(acc, acc, x1, ALU.add))
                link(V.tensor_tensor_reduce(out=x1, in0=acc, in1=acc, scale=1.0, scalar=0.0, op0=ALU.mult, op1=ALU.add,
                                            accum_out=small[:, 2:3]))
                signal(V.tensor_scalar(small[:, 0:1], small[:, 2:3], 1.0 / D, EPS, ALU.mult, ALU.add), f_ms, nth)
                dve.wait_ge(f_rs, nth)
                link(V.reciprocal(small[:, 3:4], small[:, 1:2]))
                link(V.scalar_tensor_tensor(x1, acc, small[:, 3:4], gain, ALU.mult, ALU.mult))
                dve.sem_inc(y_ready, 1)

            def qkv(p):
                n = ATT_BLOCKS[p]

                def unit(x):
                    c, lb = x // n, x % n
                    dve.wait_ge(bank_free, U_QKV[p] + x + NB + 1)
                    if c < NORMED:
                        head_norm(NORMED * p + x, lb, 4 if c < 2 else 2, qgain if c < 2 else kgain)
                    if c:
                        dve.wait_ge(zo_out[lb if p else SB], 16 * c)
                    heads = (4, 4, 2, 4, 4, 4, 4, 0, 0)[c]
                    finish(Z0[p] + x, lb, heads if p else 0, zo(p, c, lb))

                dve.wait_ge(qk_tab, 32 + (32 + 32 * SB if p else 0))
                link(V.memset(small[:, 28:32], 0.0))
                c = 0
                while c < QKV_CH:
                    if p and c in QKV_STEPS:
                        step = QKV_STEPS[c]
                        peer_step(0, step, step % 2, step, during=lambda k: unit(c * n + k // 4) if k % 4 == 3 else None)
                        c += 2
                    else:
                        for lb in range(n):
                            unit(c * n + lb)
                        if p == 0 and c % 2 == 0 and c < 2 * SB:
                            norm(nrm[3], 3, c // 2 + 1, 0)
                        c += 1

            def attention(p):
                a = att[p]
                T, blocks = (SB + 1, SB) if p else (1, 1)

                def weights(sc):
                    return zt_f[:, (sc % 4) * 640:(sc % 4) * 640 + T * P]

                for b in range(blocks):
                    qb = b + p

                    def maxes(sc):
                        dve.wait_ge(a["sc"], qb * 16 + sc + 1)
                        lo = (sc % 2) * 1024
                        link(V.tensor_reduce(small[:, 32 + sc % 4:33 + sc % 4], ps[:, lo:lo + T * P], AX.X, ALU.max))
                        signal(V.tensor_scalar(small[:, 16 + sc % 4:17 + sc % 4], small[:, 32 + sc % 4:33 + sc % 4], -SCALE, None, ALU.mult),
                               a["nm"], qb * 16 + sc + 1)

                    def inv(sc):
                        return small[:, 40 + sc % 8:41 + sc % 8]

                    def normed(sc):
                        dve.wait_ge(a["ex"], qb * 16 + sc + 3)
                        rec = V.reciprocal(inv(sc), small[:, 20 + sc % 4:21 + sc % 4])
                        if sc < 8:
                            rec.then_inc(a["pn"], 1)
                        elif sc % 2 == 0:
                            link(rec)
                        else:
                            link(rec)
                            link(V.tensor_tensor(inv(sc), inv(sc), small[:, 20 + (sc - 1) % 4:21 + (sc - 1) % 4], ALU.mult))
                            link(V.tensor_scalar(inv(sc), inv(sc), small[:, 6:7], None, ALU.mult))
                            V.scalar_tensor_tensor(weights(sc), weights(sc), inv(sc), weights(sc - 1), ALU.mult, ALU.add).then_inc(a["pn"], 1)

                    def out(o, qb=qb):
                        dve.wait_ge(a["pv"], qb * 12 + o + 3)
                        dve.wait_ge(a["pn"], qb * 12 + o + 1)
                        if o == 0 and b:
                            dve.wait_ge(a["st"], qb * 16)
                        elif o == 0:
                            for blk in range(SB) if p else ():
                                dve.wait_ge(zo_out[blk], 16 * QKV_CH)
                        c0, n = (o * HD, HD) if o < 8 else (QH * HD + (o - 8) * VD, VD)
                        V.tensor_scalar(onat[:, c0:c0 + n], bank(6 + o % 2, n), inv(o if o < 8 else 2 * o - 8), None, ALU.mult).then_inc(a["oe"], 1)

                    def end(qb):
                        dve.wait_ge(a["oe"], qb * 12 + 14)
                        od = onat[:, QH * HD:D]
                        link(V.tensor_tensor(tmp4, od, od, ALU.mult))
                        link(V.tensor_reduce(small[:, 28:32], hview(tmp4, DH), AX.X, ALU.add))
                        signal(V.tensor_scalar(small[:, 8:12], small[:, 28:32], 1.0 / VD, EPS, ALU.mult, ALU.add), a["ms"], qb + 1)
                        dve.wait_ge(a["rs"], qb + 1)
                        link(V.reciprocal(small[:, 24:28], small[:, 12:16]))
                        link(V.tensor_scalar(small[:, 24:28], small[:, 24:28], 1.0 - LAM_INIT, None, ALU.mult))
                        link(V.tensor_tensor(hview(od, DH), hview(od, DH), small[:, 24:28].unsqueeze(2).to_broadcast([P, DH, VD]), ALU.mult))
                        signal(V.tensor_tensor(hview(od, DH), hview(od, DH), subg.unsqueeze(1).to_broadcast([P, DH, VD]), ALU.mult),
                               a["o"], qb + 1)

                    def item(i):
                        if i == 0:
                            maxes(0)
                            maxes(1)
                            return
                        sc = i - 1
                        normed(sc)
                        if sc + 2 < 16:
                            maxes(sc + 2)
                        o = done_output(sc)
                        if o is not None and o >= 2:
                            out(o - 2)

                    def behind(k):
                        if b and k == 1:
                            out(10, qb - 1)
                            out(11, qb - 1)
                        elif b and k == 4:
                            end(qb - 1)
                        for i in range(17):
                            if att_item_tile(b, i) == k:
                                item(i)

                    if p and b < 3:
                        peer_step(0, b + 4, b % 2, b + 4, during=behind)
                    else:
                        if b:
                            out(10, qb - 1)
                            out(11, qb - 1)
                            end(qb - 1)
                        for i in range(17):
                            item(i)
                    if b == blocks - 1:
                        out(10)
                        out(11)
                        end(qb)

            for g in range(3):
                n, G, R = GROUP[g], grp[g], grp[g]["again"]
                if g < 2:
                    qkv(g)
                    attention(g)

                def merge(c):
                    u = c * (4 * n) + U_BR[g]
                    for lb in range(n):
                        dve.wait_ge(bank_free, u + (2 * n + lb + NB + 1))
                        link(V.tensor_tensor(zn(lb * CH, CH), zn(lb * CH, CH), zt[:, lb % ZTS[g]], ALU.mult))
                        dve.sem_inc(G["zt"], 1)
                    for lb in range(n):
                        gb = zn((SB + lb) * CH, CH)
                        dve.wait_ge(bank_free, u + (3 * n + lb + NB + 1))
                        link(V.tensor_tensor(gb, gb, zt[:, (n + lb) % ZTS[g]], ALU.mult))
                        dve.sem_inc(G["zt"], 1)
                        signal(V.tensor_tensor(zn(lb * CH, CH), zn(lb * CH, CH), gb, ALU.add), G["br"], c * n + (R * DCH + lb + 1))
                    stored(G["br_st"], c * 16 + (16 * DCH * R + 16))
                    dve.sem_inc(G["gates"], n)

                def residual(v):
                    c, lb = v // n, v % n
                    dve.wait_ge(bank_free, U_OUT[g] + v + NB + 1)
                    link(V.tensor_tensor(zt[:, v % 4], zt[:, v % 4], zn(c * CH, CH), ALU.mult))
                    dve.wait_ge(G["xt"][lb], 16 * (R * DCH + c + 1))
                    signal(V.tensor_tensor(zt[:, v % 4], zt[:, v % 4], zn(D + lb * CH, CH), ALU.add), G["ou"], R * DCH + v + 1)

                if g == 0:
                    with ch.loop(DCH, 2 * n) as c:
                        merge(c)
                elif g == 1:
                    peer_step(0, 7, 1, 7, ahead=False, during=lambda k: merge(k // 8) if k % 8 == 7 else None)
                    dve.wait_ge(fa_in, 48)
                    final(ac(A1 + 2 * D, D), ac(A1 + 3 * D, D), ac(A1, D), 1)
                else:
                    with ch.loop(DCH // 2, 2 * (STEP + 2 * n)) as i:
                        for j in range(2):
                            peer_step(1, i * 2 + (PH + j), j, i * 2 + (PH + j))
                            merge(i * 2 + j)
                dve.wait_ge(G["g1"], 16 * (1 + R))
                if g < 2:
                    for v in range(DCH * n):
                        residual(v)
                    norm(nrm[g], g, 0, T_H[g])
                    link(V.memset(acc, 0.0))
                    choose(STEP0[g], 0)
                    if g == 0:
                        dve.sem_inc(ring_free[0], RINGS[0])
                else:
                    half_ = DCH * n // 2
                    for j in range(2):
                        peer_step(1, PH + 4 + j, j, PH + 4 + j,
                                  during=lambda k: residual(j * half_ + k // 5 - 1) if k and k % 5 == 0 else None)
                    peer_step(1, PH + 6, 0, PH + 6, during=lambda k: norm(nrm[2], 2, (k - 1) // 4, T_H[2]) if k in (1, 5, 9) else None)
                    peer_step(1, PH + 7, 1, PH + 7, ahead=False)

            choose(2 * PH, 0)
            dve.wait_ge(grp[2]["sk"], DCH * GROUP[2])
            dve.sem_inc(ring_free[1], RINGS[1])
            dve.wait_ge(fa_in, 96)
            final(ac(A1, D), ac(A1 + D, D), ac(A1 + 2 * D, D), 2)
            start = ch.base + ch.k
            per_block = PH * STEP + 2 + 5
            with dve.Fori(0, GROUP[2]) as b:
                ch.base, ch.k = b * per_block + start, 0
                dve.wait_ge(hn_in, b * 16 + 16)
                link(V.tensor_copy(hcur, ac(2 * D, D)))
                dve.sem_inc(h_taken, 1)
                link(V.memset(acc, 0.0))
                dve.nop(nofuse=True)
                with dve.Fori(0, PH // 2) as hp:
                    for q in range(2):
                        ch.base, ch.k = b * per_block + start + 2 + hp * (2 * STEP) + q * STEP, 0
                        m = b * PH + hp * 2 + q
                        peer_step(2, m + 2 * PH, q, m)
                        assert ch.k == STEP
                ch.base, ch.k = b * per_block + start + 2 + PH * STEP, 0
                dve.wait_ge(fx_in, b * 16 + 32)
                final(ac(0, D), ac(D, D), ac(A1 + 2 * D, D), b + 3)
                assert ch.k == 5


_INS = ["x_prompt", "x_sample", "c", "cache_gqa_k", "cache_gqa_v", "cache_diff_k", "cache_diff_v", "c_ctx", "w_ada", "b_ada",
        "norm1_g", "norm2_g", "w_in", "q_norm_g", "k_norm_g", "lambda_q1", "lambda_k1", "lambda_q2", "lambda_k2",
        "diff_subln_g", "w_branch_a", "w_branch_b", "w_out", "peer_w_query", "peer_sub_keys", "peer_u", "peer_v",
        "final_norm_g"]
_OUTS = [(1, SEQ, D), (1, DEC_SEQ, D), (1, 1, SEQ, KVH, HD), (1, 1, SEQ, KVH, HD), (1, 1, SEQ, DH, 2, HD), (1, 1, SEQ, DH, VD)]


def rope_tables():
    f = np.float32
    rows = DEC_SEQ // GRID_W
    row = np.repeat(np.arange(rows, dtype=f), GRID_W)
    col = np.tile(np.arange(GRID_W, dtype=f), rows)
    pairs = HD // 4
    inv = np.power(f(10000.0), -np.arange(pairs, dtype=f) / f(pairs)).astype(f)
    ar, ac = row[:, None] * inv, col[:, None] * inv
    ang = np.concatenate([ar, ar, ac, ac], axis=-1)
    sign = np.repeat(np.array([-1, 1, -1, 1], f), pairs)
    return np.cos(ang).astype(f), (np.sin(ang) * sign).astype(f)


def kernel(**inputs):
    import concourse.bacc as bacc
    from concourse.bass_utils import run_bass_kernel_spmd

    nc = bacc.Bacc("TRN2", target_bir_lowering=False, num_devices=1)
    arrays, I = {}, {}
    cos, sin = rope_tables()
    for name, a in [(n, np.ascontiguousarray(inputs[n])) for n in _INS] + [("rope_cos", cos), ("rope_sin", sin)]:
        arrays[f"in_{name}"] = a
        I[name] = nc.dram_tensor(f"in_{name}", a.shape, mybir.dt.from_np(a.dtype), kind="ExternalInput").ap()
    O = [nc.dram_tensor(f"out_{i}", s, mybir.dt.float32, kind="ExternalOutput").ap() for i, s in enumerate(_OUTS)]
    build(nc, I, O)
    r = run_bass_kernel_spmd(nc, [arrays], core_ids=[0])
    return tuple(r.results[0][f"out_{i}"] for i in range(len(_OUTS)))
```
